# Optimizing a Trainium2 kernel written in Bass

```python
import math
import jax, jax.numpy as jnp
from jax import lax
import numpy as np

D_MODEL = 1024
BATCH = 1
SEQ = 256
DEPTH = 1

CONV_WIDTH = D_MODEL // 2
CONV_K = 3
N_HEADS = 8
HEAD_DIM = 64
ATTN_WIDTH = N_HEADS * HEAD_DIM
MOBA_BLOCK = 256
MOBA_TOPK = 3
QUERY_CHUNK = 32
N_BUCKETS = 32
MAX_DISTANCE = 1024
D_FF = 4 * D_MODEL
RMS_EPS = 1e-6
N_IN = 3 * CONV_WIDTH + 3 * ATTN_WIDTH + 2 * D_MODEL
NEG = -1e30

kernel_name = "hybrid_shortconv_moba_sqrelu_block"

def rms_norm(x, g):
    x32 = x.astype(jnp.float32)
    y = x32 * lax.rsqrt(jnp.mean(jnp.square(x32), axis=-1, keepdims=True) + RMS_EPS)
    return (y * g.astype(jnp.float32)).astype(x.dtype)

def t5_causal_bucket(rel):
    n = jnp.maximum(rel, 0)
    max_exact = N_BUCKETS // 2
    nf = jnp.maximum(n, max_exact).astype(jnp.float32)
    large = max_exact + (jnp.log(nf / max_exact) / math.log(MAX_DISTANCE / max_exact)
                         * (N_BUCKETS - max_exact)).astype(jnp.int32)
    large = jnp.minimum(large, N_BUCKETS - 1)
    return jnp.where(n < max_exact, n, large)

def short_conv(u, w):
    return lax.conv_general_dilated(
        u, w[:, None, :], window_strides=(1,), padding=[(CONV_K - 1, 0)],
        dimension_numbers=("NWC", "WIO", "NWC"), feature_group_count=u.shape[-1])

def moba_attention(q, k, v, rel_bias):
    b, s, h, d = q.shape
    n_blocks = max(-(-s // MOBA_BLOCK), MOBA_TOPK)
    s_pad = n_blocks * MOBA_BLOCK
    q = q.transpose(0, 2, 1, 3)
    pad = ((0, 0), (0, 0), (0, s_pad - s), (0, 0))
    k = jnp.pad(k.transpose(0, 2, 1, 3), pad)
    v = jnp.pad(v.transpose(0, 2, 1, 3), pad)
    k_blocks = k.reshape(b, h, n_blocks, MOBA_BLOCK, d)
    v_blocks = v.reshape(b, h, n_blocks, MOBA_BLOCK, d)
    k_mean = jnp.mean(k_blocks, axis=3)
    scale = HEAD_DIM ** -0.5
    bi = jnp.arange(b)[:, None, None, None]
    hi = jnp.arange(h)[None, :, None, None]
    blk_ids = jnp.arange(n_blocks)
    offs = jnp.arange(MOBA_BLOCK)
    n_sel = MOBA_TOPK * MOBA_BLOCK

    def chunk(c):
        start = c * QUERY_CHUNK
        blk = start // MOBA_BLOCK
        qc = lax.dynamic_slice_in_dim(q, start, QUERY_CHUNK, axis=2)
        qpos = start + jnp.arange(QUERY_CHUNK)
        gate = jnp.einsum('bhqd,bhnd->bhqn', qc, k_mean).astype(jnp.float32)
        gate = jnp.where(blk_ids < blk, gate, NEG)
        _, sel = lax.top_k(gate, MOBA_TOPK)
        sel_valid = sel < blk
        kg = k_blocks[bi, hi, sel]
        vg = v_blocks[bi, hi, sel]
        kpos = sel[..., None] * MOBA_BLOCK + offs
        rel = qpos[None, None, :, None, None] - kpos
        bias_past = rel_bias[hi[..., None], t5_causal_bucket(rel)]
        s_past = jnp.einsum('bhqd,bhqjkd->bhqjk', qc, kg).astype(jnp.float32) * scale + bias_past
        s_past = jnp.where(sel_valid[..., None], s_past, NEG).reshape(b, h, QUERY_CHUNK, n_sel)
        kb = lax.dynamic_slice_in_dim(k, blk * MOBA_BLOCK, MOBA_BLOCK, axis=2)
        vb = lax.dynamic_slice_in_dim(v, blk * MOBA_BLOCK, MOBA_BLOCK, axis=2)
        rel_own = qpos[:, None] - (blk * MOBA_BLOCK + offs)[None, :]
        bias_own = rel_bias[:, t5_causal_bucket(rel_own)]
        s_own = jnp.einsum('bhqd,bhkd->bhqk', qc, kb).astype(jnp.float32) * scale + bias_own
        s_own = jnp.where(rel_own >= 0, s_own, NEG)
        p = jax.nn.softmax(jnp.concatenate([s_past, s_own], axis=-1), axis=-1).astype(v.dtype)
        p_past = p[..., :n_sel].reshape(b, h, QUERY_CHUNK, MOBA_TOPK, MOBA_BLOCK)
        p_own = p[..., n_sel:]
        return (jnp.einsum('bhqjk,bhqjkd->bhqd', p_past, vg)
                + jnp.einsum('bhqk,bhkd->bhqd', p_own, vb))

    outs = lax.map(chunk, jnp.arange(s // QUERY_CHUNK))
    return outs.transpose(1, 0, 3, 2, 4).reshape(b, s, h * d)

def setup_inputs(seed: int = 0) -> dict:
    key = jax.random.key(seed)
    ks = jax.random.split(key, 14)
    nrm = jax.random.normal
    f32 = jnp.float32

    def gain(k):
        return 1.0 + 0.02 * nrm(k, (DEPTH, D_MODEL), f32)

    return {
        "x": nrm(ks[0], (BATCH, SEQ, D_MODEL), f32),
        "ln_mix_pre": gain(ks[1]),
        "w_in": nrm(ks[2], (DEPTH, D_MODEL, N_IN), f32) * D_MODEL ** -0.5,
        "conv_w": nrm(ks[3], (DEPTH, CONV_K, CONV_WIDTH), f32) * CONV_K ** -0.5,
        "w_conv_out": nrm(ks[4], (DEPTH, CONV_WIDTH, D_MODEL), f32) * CONV_WIDTH ** -0.5,
        "w_attn_out": nrm(ks[5], (DEPTH, ATTN_WIDTH, D_MODEL), f32) * ATTN_WIDTH ** -0.5,
        "rel_bias": 0.2 * nrm(ks[6], (N_HEADS, N_BUCKETS), f32),
        "w_o": nrm(ks[7], (DEPTH, D_MODEL, D_MODEL), f32) * D_MODEL ** -0.5,
        "ln_mix_post": gain(ks[8]),
        "ln_mlp_pre": gain(ks[9]),
        "w_mlp_in": nrm(ks[10], (DEPTH, D_MODEL, D_FF), f32) * D_MODEL ** -0.5,
        "w_mlp_out": nrm(ks[11], (DEPTH, D_FF, D_MODEL), f32) * D_FF ** -0.5,
        "ln_mlp_post": gain(ks[12]),
    }

def reference(x, ln_mix_pre, w_in, conv_w, w_conv_out, w_attn_out, rel_bias, w_o,
              ln_mix_post, ln_mlp_pre, w_mlp_in, w_mlp_out, ln_mlp_post):
    b, s, _ = x.shape
    c, a, dm = CONV_WIDTH, ATTN_WIDTH, D_MODEL
    splits = [c, 2 * c, 3 * c, 3 * c + a, 3 * c + 2 * a, 3 * c + 3 * a, 3 * c + 3 * a + dm]
    for l in range(DEPTH):
        h = rms_norm(x, ln_mix_pre[l])
        proj = h @ w_in[l]
        xin, gb, gc, q, k, v, g_conv, g_attn = jnp.split(proj, splits, axis=-1)
        y_c = (gb * short_conv(gc * xin, conv_w[l])) @ w_conv_out[l]
        att = moba_attention(q.reshape(b, s, N_HEADS, HEAD_DIM),
                             k.reshape(b, s, N_HEADS, HEAD_DIM),
                             v.reshape(b, s, N_HEADS, HEAD_DIM), rel_bias)
        y_a = att @ w_attn_out[l]
        m = jax.nn.sigmoid(g_conv) * y_c + jax.nn.sigmoid(g_attn) * y_a
        x = x + rms_norm(m @ w_o[l], ln_mix_post[l])
        h = rms_norm(x, ln_mlp_pre[l])
        f = jnp.square(jax.nn.relu(h @ w_mlp_in[l])) @ w_mlp_out[l]
        x = x + rms_norm(f, ln_mlp_post[l])
    return x


_drawn_inputs = setup_inputs


def setup_inputs(seed=0):
    import zlib

    import numpy as np

    out = dict(_drawn_inputs(seed))
    spreads = {}
    factors = {'ln_mix_post': 30.489, 'ln_mlp_pre': 40.411, 'ln_mlp_post': 62.36}
    for name, (base, spread) in spreads.items():
        noise = np.random.default_rng([zlib.crc32(name.encode()), seed]).standard_normal(out[name].shape)
        drawn = base * np.exp(spread * noise) if base else spread * noise
        out[name] = __import__('jax').numpy.asarray(drawn.astype(out[name].dtype))
    for name, factor in factors.items():
        out[name] = (out[name] * factor).astype(out[name].dtype)
    return out
```

```python
from contextlib import ExitStack

import numpy as np

import concourse.bass as bass
from concourse import mybir

F32 = mybir.dt.float32
F32R = mybir.dt.float32r
ACT = mybir.ActivationFunctionType
ALU = mybir.AluOpType

P = 128
EPS = 1e-6
NEG = -1e30
MAX_DISTANCE = 1024


def bucket_runs(seq, n_buckets):
    exact = n_buckets // 2
    n = np.arange(seq)
    far = np.maximum(n, exact).astype(np.float32)
    large = exact + (np.log(far / np.float32(exact)) / np.float32(np.log(MAX_DISTANCE / exact))
                     * np.float32(n_buckets - exact)).astype(np.int32)
    bucket = np.where(n < exact, n, np.minimum(large, n_buckets - 1))
    return [(int(b), int(n[bucket == b][0]), int(n[bucket == b][-1]) + 1) for b in np.unique(bucket)]


def hybrid_layer(nc, x, ln_mix_pre, w_in, conv_w, w_conv_out, w_attn_out, rel_bias, w_o,
                 ln_mix_post, ln_mlp_pre, w_mlp_in, w_mlp_out, ln_mlp_post, out):
    SEQ, D = x.shape[1], x.shape[2]
    H, NBUCKETS = rel_bias.shape
    C = conv_w.shape[2]
    HD = C // H
    D_FF = w_mlp_in.shape[2]
    NT = SEQ // P
    KD, KC = D // P, C // P
    W = 512
    HALF_K = 4
    HALF = HALF_K * W
    SLOTS = 4
    N_PROJ = w_in.shape[2] // W
    N_FF = D_FF // W
    SCALE = float(HD) ** -0.5
    TWO = 2 * P
    ROW = 3 * P
    assert (NT, KD, KC, D // W, C, N_PROJ) == (2, 8, 4, 2, W, 10)

    J_BRANCH = 2 * N_PROJ
    J_O = J_BRANCH + 4
    J_MLP = J_O + 4
    N_HALVES = J_MLP + 4 * N_FF
    XIN, GB, GC, Q, K, V = 0, 1, 2, 3, 4, 5
    ORDER = [Q, K, V, XIN, GC, GB, 6, 7, 8, 9]
    STEP_XIN, STEP_C, STEP_B, STEP_GATES = 3, 4, 5, 6
    ATT0 = 5

    x_v = x.rearrange("b (t p) d -> (b p) t d", p=P)
    out_v = out.rearrange("b (t p) d -> (b p) t d", p=P)
    w_in_v = w_in[0].rearrange("(k p) n -> p k n", p=P)
    w_co_v = w_conv_out[0].rearrange("(k p) n -> p k n", p=P)
    w_ao_v = w_attn_out[0].rearrange("(k p) n -> p k n", p=P)
    w_o_v = w_o[0].rearrange("(k p) n -> p k n", p=P)
    w_up_v = w_mlp_in[0].rearrange("(k p) n -> p k n", p=P)
    w_down_v = w_mlp_out[0].rearrange("(g k p) n -> p g k n", p=P, k=KC)
    bias_rows_dram = nc.dram_tensor("bias_rows_dram", (H, ROW), F32, kind="Internal")

    ctx = ExitStack()
    with ctx:
        def sb(name, shape, dt=F32):
            return ctx.enter_context(nc.sbuf_tensor(name, shape, dt))

        def psum(name):
            return ctx.enter_context(nc.psum_tensor(name, [P, W], F32))

        def sem(name):
            return ctx.enter_context(nc.semaphore(name))

        w_raw = sb("w_raw", [P, SLOTS, HALF])
        w_hi = sb("w_hi", [P, SLOTS, HALF], F32R)
        w_lo = sb("w_lo", [P, SLOTS, HALF], F32R)
        resid = sb("resid", [P, NT, D])
        rows = sb("rows", [P, NT, D])
        inT_hi = sb("inT_hi", [P, KD, SEQ], F32R)
        inT_lo = sb("inT_lo", [P, KD, SEQ], F32R)
        midT_hi = sb("midT_hi", [P, KC, SEQ], F32R)
        midT_lo = sb("midT_lo", [P, KC, SEQ], F32R)
        attT_hi = sb("attT_hi", [P, KC, SEQ], F32R)
        attT_lo = sb("attT_lo", [P, KC, SEQ], F32R)
        gates = sb("gates", [P, NT, 2 * D])
        bufA = sb("bufA", [P, NT, W])
        bufB = sb("bufB", [P, NT, W])
        bufC = sb("bufC", [P, NT, W])
        bufQT = sb("bufQT", [P, KC, SEQ])
        bufKT = sb("bufKT", [P, KC, SEQ])
        bufV = sb("bufV", [P, NT, W])
        q_tok, xin_tok = bufA, bufA
        k_tok, u_tok = bufB, bufB
        conv = bufB[:].rearrange("p t w -> p (t w)").rearrange("p (c s) -> p c s", c=KC)
        gb_tok, att_tok, hidden = bufC, bufC, bufC
        hidden0 = gates[:, :, 0:W]
        squares = gates[:, :, D:2 * D]
        qT, kT, v_tok = bufQT, bufKT, bufV
        g_post = bufQT[:].rearrange("p c s -> p (c s)")
        g_mlp = bufKT[:].rearrange("p c s -> p (c s)")
        g_last = bufV[:].rearrange("p t w -> p (t w)")
        uT = sb("uT", [P, KC, 2 + SEQ])
        bias = sb("bias", [P, H, TWO])
        probs = sb("probs", [P, 2, 3 * P])
        probsT = sb("probsT", [P, 2, 3 * P])
        bias_row = gates[0:H, 0, 0:ROW]
        bias_tab = gates[0:H, 0, W - 2 * NBUCKETS:W]
        conv_rows = gates[0:3 * KC, 0, W:W + P]
        gain_row = gates[0:1, 1, 0:D]
        ones_row = sb("ones_row", [1, P])
        conv_taps = sb("conv_taps", [P, 3 * KC])
        ident = sb("ident", [P, P])
        neg_max = sb("neg_max", [P, NT, H])
        den = sb("den", [P, NT, H])
        rden = sb("rden", [P, NT, H])
        ss = sb("ss", [P, 16])
        var = sb("var", [P, 8])
        std = sb("std", [P, 8])
        newton = sb("newton", [P, 8])
        inv0 = sb("inv0", [P, 8])
        inv = sb("inv", [P, 8])

        acc = [psum("acc0"), psum("acc1")]
        score_ps = psum("score_ps")
        probT_ps = psum("probT_ps")
        att_ps = [psum("att0"), psum("att1")]
        tr = [psum("tr0"), psum("tr1")]
        branch_ps = [(acc[0], acc[1]), (score_ps, probT_ps)]
        mix_ps = [(acc[0], acc[1]), (score_ps, probT_ps)]
        down_ps = [(att_ps[0], att_ps[1]), (score_ps, probT_ps)]

        x_loaded = [sem(f"x_loaded{t}") for t in range(NT)]
        gain_row_loaded = sem("gain_row_loaded")
        conv_w_loaded = sem("conv_w_loaded")
        rel_bias_loaded = sem("rel_bias_loaded")
        half_loaded = [sem(f"half_loaded{s}") for s in range(SLOTS)]
        bias_rows_stored = sem("bias_rows_stored")
        bias_loaded = sem("bias_loaded")
        gains_loaded = [sem(f"gains_loaded{i}") for i in range(3)]
        stored = sem("stored")
        pool_seq = sem("pool_seq")
        consts_ready = sem("consts_ready")
        bias_row_ready = sem("bias_row_ready")
        half_hi = sem("half_hi")
        half_lo = sem("half_lo")
        halves_used = sem("halves_used")
        dve_seq = sem("dve_seq")
        gain_spread = sem("gain_spread")
        taps_transposed = sem("taps_transposed")
        taps_ready = sem("taps_ready")
        xg_ready = sem("xg_ready")
        squared = sem("squared")
        var_ready = sem("var_ready")
        std_ready = sem("std_ready")
        inv_ready = sem("inv_ready")
        inT_psum = sem("inT_psum")
        inT_hi_ready = sem("inT_hi_ready")
        inT_lo_ready = sem("inT_lo_ready")
        tile0_done = sem("tile0_done")
        proj_taken = [sem(f"proj_taken{t}") for t in range(NT)]
        head_psum = sem("head_psum")
        head_taken = sem("head_taken")
        scores_ready = sem("scores_ready")
        scores_biased = sem("scores_biased")
        probs_ready = sem("probs_ready")
        probsT_psum = sem("probsT_psum")
        probsT_ready = sem("probsT_ready")
        pv_done = sem("pv_done")
        att_ready = sem("att_ready")
        convT_psum = sem("convT_psum")
        uT_ready = sem("uT_ready")
        y_ready = sem("y_ready")
        y_hi_ready = sem("y_hi_ready")
        y_lo_ready = sem("y_lo_ready")
        attT_psum = sem("attT_psum")
        attT_hi_ready = sem("attT_hi_ready")
        attT_lo_ready = sem("attT_lo_ready")
        branch_done = sem("branch_done")
        gated = sem("gated")
        m_ready = sem("m_ready")
        mix_gained = sem("mix_gained")
        resid_ready = sem("resid_ready")
        h_ready = sem("h_ready")
        relu_done = sem("relu_done")
        hidden_ready = sem("hidden_ready")
        hiddenT_psum = sem("hiddenT_psum")
        hiddenT_hi = sem("hiddenT_hi")
        hiddenT_lo = sem("hiddenT_lo")
        down_done = sem("down_done")
        down_gained = sem("down_gained")
        out_ready = sem("out_ready")

        block = ctx.enter_context(nc.Block())

        @block.sync
        def _(sp):
            def load_half(j, slot, src, cols=W):
                if not isinstance(j, int) or j >= SLOTS:
                    sp.wait_ge(half_lo, j - (SLOTS - 1))
                sp.dma_start(w_raw[:, slot, :].rearrange("p (k n) -> p k n", n=cols), src).then_inc(
                    half_loaded[slot], 16)

            def load_square_half(j, w_v, n, h):
                load_half(j, j % SLOTS, w_v[:, h * HALF_K:(h + 1) * HALF_K, n * W:(n + 1) * W])

            sp.dma_start(resid[:, 0, :], x_v[:, 0, :]).then_inc(x_loaded[0], 16)
            sp.dma_start(gain_row[:], ln_mix_pre).then_inc(gain_row_loaded, 16)
            load_square_half(0, w_in_v, ORDER[0], 0)
            sp.dma_start(resid[:, 1, :], x_v[:, 1, :]).then_inc(x_loaded[1], 16)
            load_square_half(1, w_in_v, ORDER[0], 1)
            sp.dma_start(conv_rows[:], conv_w[0].rearrange("j (c p) -> (j c) p", p=P)).then_inc(conv_w_loaded, 16)
            sp.dma_start(bias_tab[:, 0:NBUCKETS], rel_bias).then_inc(rel_bias_loaded, 16)
            for j in range(2, 8):
                load_square_half(j, w_in_v, ORDER[j // 2], j % 2)
            sp.wait_ge(bias_row_ready, 1)
            sp.dma_start(bias_rows_dram.ap(), bias_row[:]).then_inc(bias_rows_stored, 16)
            sp.wait_ge(bias_rows_stored, 16)
            sp.dma_start(bias[:], bass.AP(tensor=bias_rows_dram, offset=0,
                                          ap=[[1, P], [ROW, H], [1, TWO]])).then_inc(bias_loaded, 16)
            for j in range(8, J_BRANCH):
                load_square_half(j, w_in_v, ORDER[j // 2], j % 2)
            for n in range(2):
                load_square_half(J_BRANCH + 2 * n, w_co_v, n, 0)
                load_square_half(J_BRANCH + 2 * n + 1, w_ao_v, n, 0)
            sp.wait_ge(pv_done, H)
            for i, (dst, gain) in enumerate(((g_post, ln_mix_post), (g_mlp, ln_mlp_pre), (g_last, ln_mlp_post))):
                sp.dma_start(dst, gain[0].partition_broadcast(P)).then_inc(gains_loaded[i], 16)
            for n in range(2):
                for h in range(2):
                    load_square_half(J_O + 2 * n + h, w_o_v, n, h)
            for g in range(2):
                for h in range(2):
                    load_square_half(J_MLP + 2 * g + h, w_up_v, g, h)

            def load_down(j, g, slot0):
                for h in range(2):
                    src = w_down_v[:, bass.ts(g, 1), 2 * h:2 * h + 2, :].rearrange("p g k n -> p (g k) n")
                    load_half(j + h, slot0 + h, src, cols=D)

            def load_up(j, g, slot0):
                for h in range(2):
                    load_half(j + h, slot0 + h, w_up_v[:, h * HALF_K:(h + 1) * HALF_K, bass.ts(g, W)])

            load_down(J_MLP + 4, 0, 0)
            load_up(J_MLP + 6, 2, 2)
            with sp.Fori(0, N_FF - 3) as i:
                load_down(4 * i + J_MLP + 8, i + 1, 0)
                load_up(4 * i + J_MLP + 10, i + 3, 2)
            load_down(N_HALVES - 4, N_FF - 2, 0)
            load_down(N_HALVES - 2, N_FF - 1, 2)
            for t in range(NT):
                for n in range(2):
                    sp.wait_ge(out_ready, 2 * t + n + 1)
                    sp.dma_start(out_v[:, t, n * W:(n + 1) * W], rows[:, t, n * W:(n + 1) * W]).then_inc(stored, 16)
            sp.wait_ge(stored, 16 * 2 * NT)

        @block.gpsimd
        def _(pool):
            seq = [0]

            def link(ins):
                seq[0] += 1
                ins.then_inc(pool_seq, 1)
                pool.wait_ge(pool_seq, seq[0])

            link(nc.gpsimd.memset(ident[:], 0.0))
            nc.gpsimd.affine_select(out=ident[:], in_=ident[:], compare_op=ALU.not_equal, fill=1.0, base=0,
                                    pattern=[[-1, P]], channel_multiplier=1).then_inc(consts_ready, 1)
            nc.gpsimd.memset(ones_row[:], 1.0).then_inc(consts_ready, 1)
            nc.gpsimd.memset(uT[:, :, 0:2], 0.0).then_inc(consts_ready, 1)
            link(nc.gpsimd.memset(bias_row[:], NEG / SCALE))
            pool.wait_ge(rel_bias_loaded, 16)
            link(nc.gpsimd.tensor_scalar(bias_tab[:, NBUCKETS:], bias_tab[:, 0:NBUCKETS], 1.0 / SCALE, 1.0,
                                         ALU.mult, ALU.mult))
            for b, lo, hi in bucket_runs(SEQ, NBUCKETS):
                last = nc.gpsimd.tensor_copy(bias_row[:, P - 1 + lo:P - 1 + hi],
                                             bias_tab[:, NBUCKETS + b:NBUCKETS + b + 1].to_broadcast([H, hi - lo]))
            last.then_inc(bias_row_ready, 1)
            for t in range(NT):
                for n in range(2):
                    pool.wait_ge(gated, 2 * t + n + 1)
                    cols = slice(n * W, (n + 1) * W)
                    nc.gpsimd.tensor_tensor(rows[:, t, cols], gates[:, t, cols], gates[:, t, D + n * W:D + (n + 1) * W],
                                            ALU.add).then_inc(m_ready, 1)

        @block.scalar
        def _(act):
            def split_hi(j, slot, used):
                act.wait_ge(half_loaded[slot], used)
                if not isinstance(j, int) or j >= SLOTS:
                    act.wait_ge(halves_used, j - (SLOTS - 1))
                nc.scalar.copy(w_hi[:, slot, :], w_raw[:, slot, :]).then_inc(half_hi, 1)

            def split_half(j):
                split_hi(j, j % SLOTS, 16 * (j // SLOTS + 1))

            def inT_hi_tile(t, count):
                act.wait_ge(inT_psum, count)
                for b in range(2):
                    ins = nc.scalar.copy(inT_hi[:, 4 * b:4 * b + 4, t * P:(t + 1) * P],
                                         (tr if count != 2 else [score_ps, probT_ps])[b][:].rearrange("p (k s) -> p k s", s=P))
                    ins.then_inc(inT_hi_ready, 1)

            def root(col, count, width=1):
                act.wait_ge(var_ready, count)
                nc.scalar.activation(std[:, col:col + width], var[:, col:col + width], ACT.Sqrt).then_inc(std_ready, 1)

            inT_hi_tile(0, 1)
            split_half(0)
            split_half(1)
            inT_hi_tile(1, 2)
            for t in range(NT):
                act.wait_ge(x_loaded[t], 16)
                nc.scalar.activation(squares[:, t, :], resid[:, t, :], ACT.Square,
                                     accum_out=ss[:, t:t + 1]).then_inc(squared, 1)
            root(0, 1, NT)
            split_half(2)
            split_half(3)
            act.wait_ge(inv_ready, 1)

            for unit in range(2 * N_PROJ):
                step, t = divmod(unit, NT)
                if t == 1:
                    split_half(2 * step + 4)
                head = unit - ATT0
                if 0 <= head < H:
                    act.wait_ge(scores_biased, head + 1)
                    for tile, cols in ((1, slice(0, TWO)), (0, slice(TWO, ROW))):
                        ins = nc.scalar.activation(probs[:, head % 2, cols], probs[:, head % 2, cols], ACT.Exp,
                                                   bias=neg_max[:, tile, head:head + 1], scale=-1.0,
                                                   accum_out=den[:, tile, head:head + 1])
                    ins.then_inc(probs_ready, 1)
                if step != STEP_C:
                    if t == 0:
                        act.wait_ge(tile0_done, step + 1)
                    else:
                        act.wait_ge(halves_used, 2 * step + 2)
                    rms = inv[:, t:t + 1]
                    if step >= STEP_GATES:
                        g = step - STEP_GATES
                        nc.scalar.activation(gates[:, t, g * W:(g + 1) * W], acc[t][:], ACT.Sigmoid,
                                             scale=rms).then_inc(proj_taken[t], 1)
                    else:
                        if step == STEP_XIN:
                            act.wait_ge(head_psum, 2)
                        dst = {0: q_tok, 1: k_tok, 2: v_tok, STEP_XIN: xin_tok, STEP_B: gb_tok}[step]
                        nc.scalar.activation(dst[:, t, :], acc[t][:], ACT.Copy, scale=rms).then_inc(proj_taken[t], 1)
                if unit == 2 * STEP_B + 3:
                    act.wait_ge(y_ready, 1)
                    nc.scalar.copy(midT_hi[:], conv).then_inc(y_hi_ready, 1)
                if unit == ATT0 + H + 3:
                    for tile in range(NT):
                        act.wait_ge(attT_psum, tile + 1)
                        nc.scalar.copy(attT_hi[:, :, tile * P:(tile + 1) * P],
                                       tr[tile][:].rearrange("p (k s) -> p k s", s=P)).then_inc(attT_hi_ready, 1)
                if t == 1:
                    split_half(2 * step + 5)

            nc.scalar.preload_act_table(ACT.Sqrt)
            inT_hi_tile(0, 3)
            for j in range(J_O, J_O + 4):
                split_half(j)
            inT_hi_tile(1, 4)

            def square_sum(src, dst, col):
                nc.scalar.activation(dst, src, ACT.Square, accum_out=ss[:, col:col + 1]).then_inc(squared, 1)

            def mix_squares(t, n):
                if t == 0:
                    act.wait_ge(tile0_done, N_PROJ + n + 1)
                else:
                    act.wait_ge(halves_used, J_O + 2 * n + 2)
                square_sum(mix_ps[t][n][:], squares[:, t, n * W:(n + 1) * W], 2 + 2 * t + n)

            def resid_squares(t):
                act.wait_ge(resid_ready, t + 1)
                square_sum(resid[:, t, :], squares[:, t, :], 6 + t)

            mix_squares(0, 0)
            mix_squares(0, 1)
            root(2, 2)
            resid_squares(0)
            root(4, 3)
            split_half(J_MLP)
            split_half(J_MLP + 1)
            mix_squares(1, 0)
            inT_hi_tile(0, 5)
            split_half(J_MLP + 2)
            mix_squares(1, 1)
            split_half(J_MLP + 3)
            root(3, 4)
            resid_squares(1)
            root(5, 5)

            def relu_squared(bank, dst, t, count):
                nc.scalar.activation(dst, bank[:], ACT.Relu, scale=inv[:, 4 + t:5 + t]).then_inc(relu_done, 1)
                act.wait_ge(relu_done, count)
                nc.scalar.activation(dst, dst, ACT.Square).then_inc(hidden_ready, 1)

            def hiddenT_hi_tile(t, count):
                act.wait_ge(hiddenT_psum, count)
                nc.scalar.copy(midT_hi[:, :, t * P:(t + 1) * P],
                               tr[t][:].rearrange("p (k s) -> p k s", s=P)).then_inc(hiddenT_hi, 1)

            act.wait_ge(inv_ready, 3)
            act.wait_ge(tile0_done, N_PROJ + 3)
            relu_squared(acc[0], hidden0[:, 0, :], 0, 1)
            inT_hi_tile(1, 6)
            act.wait_ge(tile0_done, N_PROJ + 4)
            relu_squared(acc[1], hidden[:, 0, :], 0, 2)
            act.wait_ge(inv_ready, 5)
            act.wait_ge(halves_used, J_MLP + 2)
            relu_squared(acc[0], hidden0[:, 1, :], 1, 3)
            split_half(J_MLP + 4)
            split_half(J_MLP + 5)
            hiddenT_hi_tile(0, 1)
            hiddenT_hi_tile(1, 2)
            act.wait_ge(halves_used, J_MLP + 4)
            relu_squared(acc[1], hidden[:, 1, :], 1, 4)
            split_half(J_MLP + 6)
            split_half(J_MLP + 7)
            hiddenT_hi_tile(0, 3)
            hiddenT_hi_tile(1, 4)
            with act.Fori(0, N_FF - 2) as i:
                for h in range(2):
                    split_hi(4 * i + J_MLP + 8 + h, h, 16 * i + 16 * ((J_MLP + 8) // SLOTS + 1))
                act.wait_ge(tile0_done, i + N_PROJ + 5)
                relu_squared(acc[0], hidden[:, 0, :], 0, 2 * i + 5)
                act.wait_ge(halves_used, 4 * i + J_MLP + 8)
                relu_squared(acc[1], hidden[:, 1, :], 1, 2 * i + 6)
                for h in range(2):
                    split_hi(4 * i + J_MLP + 10 + h, 2 + h, 16 * i + 16 * ((J_MLP + 10) // SLOTS + 1))
                hiddenT_hi_tile(0, 2 * i + 5)
                hiddenT_hi_tile(1, 2 * i + 6)
            for t in range(NT):
                for n in range(2):
                    act.wait_ge(down_done, 2 * t + n + 1)
                    square_sum(down_ps[t][n][:], squares[:, t, n * W:(n + 1) * W], 8 + 2 * t + n)
                root(6 + t, 6 + t)

        @block.vector
        def _(dve):
            seq = [0]

            def link(ins):
                seq[0] += 1
                ins.then_inc(dve_seq, 1)
                dve.wait_ge(dve_seq, seq[0])

            def split_lo(j, slot):
                dve.wait_ge(half_hi, j + 1)
                nc.vector.tensor_tensor(w_lo[:, slot, :], w_raw[:, slot, :], w_hi[:, slot, :].bitcast(F32),
                                        ALU.subtract).then_inc(half_lo, 1)

            def split_half(j):
                split_lo(j, j % SLOTS)

            def inT_lo_tile(t, count):
                for b in range(2):
                    dve.wait_ge(inT_hi_ready, 2 * count - 1 + b)
                    nc.vector.tensor_tensor(inT_lo[:, 4 * b:4 * b + 4, t * P:(t + 1) * P],
                                            (tr if count != 2 else [score_ps, probT_ps])[b][:].rearrange("p (k s) -> p k s", s=P),
                                            inT_hi[:, 4 * b:4 * b + 4, t * P:(t + 1) * P].bitcast(F32),
                                            ALU.subtract).then_inc(inT_lo_ready, 1)

            def variance(col, width, sums, parts, count):
                dve.wait_ge(squared, count)
                if parts == 2:
                    link(nc.vector.tensor_tensor(ss[:, 12:13], ss[:, sums:sums + 1], ss[:, sums + 1:sums + 2], ALU.add))
                    sums = 12
                nc.vector.tensor_scalar(var[:, col:col + width], ss[:, sums:sums + width], 1.0 / D, EPS,
                                        ALU.mult, ALU.add).then_inc(var_ready, 1)

            def inverse(col, width, count):
                s = slice(col, col + width)
                dve.wait_ge(std_ready, count)
                link(nc.vector.reciprocal(inv0[:, s], std[:, s]))
                link(nc.vector.tensor_tensor(newton[:, s], inv0[:, s], inv0[:, s], ALU.mult))
                link(nc.vector.tensor_tensor(newton[:, s], newton[:, s], var[:, s], ALU.mult))
                link(nc.vector.tensor_scalar(newton[:, s], newton[:, s], -0.5, 1.5, ALU.mult, ALU.add))
                nc.vector.tensor_tensor(inv[:, s], inv0[:, s], newton[:, s], ALU.mult).then_inc(inv_ready, 1)
                dve.wait_ge(inv_ready, count)

            dve.wait_ge(gain_spread, 1)
            for t in range(NT):
                dve.wait_ge(x_loaded[t], 16)
                for b in range(2):
                    nc.vector.tensor_tensor(rows[:, t, b * W:(b + 1) * W], resid[:, t, b * W:(b + 1) * W], acc[b][:],
                                            ALU.mult).then_inc(xg_ready, 1)
                if t == 0:
                    inT_lo_tile(0, 1)
                    split_half(0)
            split_half(1)
            inT_lo_tile(1, 2)
            variance(0, NT, 0, 1, 2)
            inverse(0, NT, 1)
            split_half(2)
            split_half(3)
            dve.wait_ge(taps_transposed, 1)
            nc.vector.tensor_copy(conv_taps[:], att_ps[0][:, 0:3 * KC]).then_inc(taps_ready, 1)
            dve.wait_ge(taps_ready, 1)

            def tap(j, c):
                return conv_taps[:, j * KC + c:j * KC + c + 1]

            for unit in range(2 * N_PROJ):
                step, t = divmod(unit, NT)
                if t == 1:
                    split_half(2 * step + 4)
                head = unit - ATT0
                if unit in (2, 4):
                    dve.wait_ge(head_psum, unit)
                    for tile in range(NT):
                        ins = nc.vector.tensor_copy((qT if unit == 2 else kT)[:, :, tile * P:(tile + 1) * P],
                                                    tr[tile][:].rearrange("p (k s) -> p k s", s=P))
                    ins.then_inc(head_taken, 1)
                if 0 <= head < H:
                    if head == 0:
                        dve.wait_ge(bias_loaded, 16)
                    dve.wait_ge(scores_ready, head + 1)
                    if head >= 2:
                        dve.wait_ge(probsT_psum, head - 1)
                    for tile, cols, window in ((1, slice(0, TWO), slice(TWO - 1, None, -1)),
                                               (0, slice(TWO, ROW), slice(P - 1, None, -1))):
                        ins = nc.vector.tensor_tensor_reduce(
                            out=probs[:, head % 2, cols], in0=score_ps[:, cols], in1=bias[:, head, window],
                            scale=-SCALE, scalar=3.0e38, op0=ALU.add, op1=ALU.min,
                            accum_out=neg_max[:, tile, head:head + 1])
                    ins.then_inc(scores_biased, 1)
                if 1 <= head <= H:
                    dve.wait_ge(probsT_psum, head)
                    if head >= 3:
                        dve.wait_ge(pv_done, head - 2)
                    nc.vector.tensor_copy(probsT[:, (head - 1) % 2, :], probT_ps[:, 0:ROW]).then_inc(probsT_ready, 1)
                if step == STEP_C:
                    if t == 0:
                        dve.wait_ge(tile0_done, step + 1)
                        dve.wait_ge(head_psum, 4)
                    else:
                        dve.wait_ge(halves_used, 2 * step + 2)
                    dve.wait_ge(proj_taken[t], STEP_XIN + 1)
                    nc.vector.scalar_tensor_tensor(out=u_tok[:, t, :], in0=acc[t][:], scalar=inv[:, t:t + 1],
                                                   in1=xin_tok[:, t, :], op0=ALU.mult, op1=ALU.mult).then_inc(
                                                       proj_taken[t], 1)
                if unit == 2 * STEP_B:
                    dve.wait_ge(convT_psum, 2)
                    for tile in range(NT):
                        ins = nc.vector.tensor_copy(uT[:, :, 2 + tile * P:2 + (tile + 1) * P],
                                                    tr[tile][:].rearrange("p (k s) -> p k s", s=P))
                    ins.then_inc(uT_ready, 1)
                    dve.wait_ge(uT_ready, 1)
                if unit == 2 * STEP_B + 1:
                    for c in range(KC):
                        ins = nc.vector.tensor_scalar(conv[:, c, :], uT[:, c, 2:2 + SEQ], tap(2, c), None, ALU.mult)
                    link(ins)
                    for j in (1, 0):
                        for c in range(KC):
                            ins = nc.vector.scalar_tensor_tensor(out=conv[:, c, :], in0=uT[:, c, j:j + SEQ],
                                                                 scalar=tap(j, c), in1=conv[:, c, :],
                                                                 op0=ALU.mult, op1=ALU.add)
                        link(ins)
                if unit == 2 * STEP_B + 3:
                    dve.wait_ge(convT_psum, 4)
                    for tile in range(NT):
                        half_conv = conv[:, :, tile * P:(tile + 1) * P]
                        ins = nc.vector.tensor_tensor(half_conv, tr[tile][:].rearrange("p (k s) -> p k s", s=P),
                                                      half_conv, ALU.mult)
                    ins.then_inc(y_ready, 1)
                    dve.wait_ge(y_hi_ready, 1)
                    nc.vector.tensor_tensor(midT_lo[:], conv, midT_hi[:].bitcast(F32), ALU.subtract).then_inc(y_lo_ready, 1)
                if unit == ATT0 + H + 2:
                    link(nc.vector.reciprocal(rden[:], den[:]))
                    dve.wait_ge(pv_done, H)
                    for tile in range(NT):
                        ins = nc.vector.tensor_tensor(att_tok[:, tile, :].rearrange("p (h d) -> p h d", h=H),
                                                      att_ps[tile][:].rearrange("p (h d) -> p h d", h=H),
                                                      rden[:, tile, :].unsqueeze(2).to_broadcast([P, H, HD]), ALU.mult)
                    ins.then_inc(att_ready, 1)
                if unit == ATT0 + H + 3:
                    for tile in range(NT):
                        cols = slice(tile * P, (tile + 1) * P)
                        dve.wait_ge(attT_hi_ready, tile + 1)
                        nc.vector.tensor_tensor(attT_lo[:, :, cols], tr[tile][:].rearrange("p (k s) -> p k s", s=P),
                                                attT_hi[:, :, cols].bitcast(F32), ALU.subtract).then_inc(attT_lo_ready, 1)
                if t == 1:
                    split_half(2 * step + 5)

            def gate(t, n):
                if t == 0:
                    dve.wait_ge(branch_done, n + 1)
                else:
                    dve.wait_ge(halves_used, J_BRANCH + 2 * n + 2)
                for b in range(2):
                    g = gates[:, t, b * D + n * W:b * D + (n + 1) * W]
                    ins = nc.vector.tensor_tensor(g, branch_ps[n][b][:], g, ALU.mult)
                ins.then_inc(gated, 1)

            gate(0, 0)
            gate(0, 1)
            split_half(J_O)
            split_half(J_O + 1)
            inT_lo_tile(0, 3)
            gate(1, 0)
            split_half(J_O + 2)
            gate(1, 1)
            split_half(J_O + 3)
            inT_lo_tile(1, 4)

            def mix_gain(t, n):
                dve.wait_ge(squared, 3 * t + n + 3)
                cols = slice(n * W, (n + 1) * W)
                nc.vector.tensor_tensor(rows[:, t, cols], mix_ps[t][n][:], g_post[:, cols], ALU.mult).then_inc(mix_gained, 1)

            def residual(t):
                dve.wait_ge(mix_gained, 2 * t + 2)
                nc.vector.scalar_tensor_tensor(out=resid[:, t, :], in0=rows[:, t, :], scalar=inv[:, 2 + t:3 + t],
                                               in1=resid[:, t, :], op0=ALU.mult, op1=ALU.add).then_inc(resid_ready, 1)
                dve.wait_ge(resid_ready, t + 1)
                nc.vector.tensor_tensor(rows[:, t, :], resid[:, t, :], g_mlp, ALU.mult).then_inc(h_ready, 1)

            dve.wait_ge(gains_loaded[0], 16)
            dve.wait_ge(gains_loaded[1], 16)
            mix_gain(0, 0)
            variance(2, 1, 2, 2, 4)
            mix_gain(0, 1)
            inverse(2, 1, 2)
            residual(0)
            variance(4, 1, 6, 1, 5)
            inverse(4, 1, 3)
            split_half(J_MLP)
            split_half(J_MLP + 1)
            mix_gain(1, 0)
            inT_lo_tile(0, 5)
            split_half(J_MLP + 2)
            variance(3, 1, 4, 2, 7)
            mix_gain(1, 1)
            inverse(3, 1, 4)
            residual(1)
            variance(5, 1, 7, 1, 8)
            split_half(J_MLP + 3)
            inverse(5, 1, 5)
            inT_lo_tile(1, 6)

            def hiddenT_lo_tile(t, count):
                dve.wait_ge(hiddenT_hi, count)
                nc.vector.tensor_tensor(midT_lo[:, :, t * P:(t + 1) * P], tr[t][:].rearrange("p (k s) -> p k s", s=P),
                                        midT_hi[:, :, t * P:(t + 1) * P].bitcast(F32),
                                        ALU.subtract).then_inc(hiddenT_lo, 1)

            split_half(J_MLP + 4)
            split_half(J_MLP + 5)
            hiddenT_lo_tile(0, 1)
            hiddenT_lo_tile(1, 2)
            split_half(J_MLP + 6)
            split_half(J_MLP + 7)
            hiddenT_lo_tile(0, 3)
            hiddenT_lo_tile(1, 4)
            with dve.Fori(0, N_FF - 2) as i:
                for h in range(4):
                    split_lo(4 * i + J_MLP + 8 + h, h)
                hiddenT_lo_tile(0, 2 * i + 5)
                hiddenT_lo_tile(1, 2 * i + 6)
            dve.wait_ge(gains_loaded[2], 16)
            for t in range(NT):
                for n in range(2):
                    cols = slice(n * W, (n + 1) * W)
                    if n == 0:
                        dve.wait_ge(squared, 9 + 2 * t)
                    else:
                        variance(6 + t, 1, 8 + 2 * t, 2, 10 + 2 * t)
                    nc.vector.tensor_tensor(rows[:, t, cols], down_ps[t][n][:], g_last[:, cols],
                                            ALU.mult).then_inc(down_gained, 1)
                inverse(6 + t, 1, 6 + t)
                dve.wait_ge(down_gained, 2 * t + 2)
                for n in range(2):
                    cols = slice(n * W, (n + 1) * W)
                    nc.vector.scalar_tensor_tensor(out=rows[:, t, cols], in0=rows[:, t, cols], scalar=inv[:, 6 + t:7 + t],
                                                   in1=resid[:, t, cols], op0=ALU.mult, op1=ALU.add).then_inc(out_ready, 1)

        @block.tensor
        def _(pe):
            def product(bank, a_hi, a_lo, k, t, slot, off, start, stop):
                hi, lo = a_hi[:, k, t * P:(t + 1) * P], a_lo[:, k, t * P:(t + 1) * P]
                b_hi, b_lo = w_hi[:, slot, off:off + W], w_lo[:, slot, off:off + W]
                nc.tensor.matmul(bank[:], hi, b_hi, start=start, stop=False)
                nc.tensor.matmul(bank[:], hi, b_lo, start=False, stop=False)
                return nc.tensor.matmul(bank[:], lo, b_hi, start=False, stop=stop)

            def wide_unit(bank, t, slot0, first_half, done=None, midway=None):
                for k in range(KD):
                    if t == 0 and k % HALF_K == 0:
                        pe.wait_ge(half_lo, first_half + k // HALF_K + 1)
                    if k == HALF_K and midway is not None:
                        midway()
                    last = product(bank, inT_hi, inT_lo, k, t, slot0 + k // HALF_K, k % HALF_K * W, k == 0, k == KD - 1)
                    if t == 1 and k % HALF_K == HALF_K - 1 and (done is None or k < KD - 1):
                        last.then_inc(halves_used, 1)
                if done is not None:
                    last.then_inc(done, 1)

            def transpose_rows(src, t, banks, done):
                for k in range(KD):
                    last = nc.tensor.transpose(banks[k // 4][:, k % 4 * P:(k % 4 + 1) * P],
                                               src[:, t, k * P:(k + 1) * P], ident[:])
                last.then_inc(done, 1)

            def transpose_cols(src, t, done):
                for k in range(KC):
                    last = nc.tensor.transpose(tr[t][:, k * P:(k + 1) * P], src[:, t, k * P:(k + 1) * P], ident[:])
                last.then_inc(done, 1)

            pe.wait_ge(consts_ready, 3)
            pe.wait_ge(gain_row_loaded, 16)
            for b in range(2):
                last = nc.tensor.matmul(acc[b][:], ones_row[:], gain_row[:, b * W:(b + 1) * W], start=True, stop=True)
            last.then_inc(gain_spread, 1)
            pe.wait_ge(xg_ready, 2)
            transpose_rows(rows, 0, tr, inT_psum)
            pe.wait_ge(xg_ready, 4)
            transpose_rows(rows, 1, [score_ps, probT_ps], inT_psum)
            pe.wait_ge(conv_w_loaded, 16)
            nc.tensor.transpose(att_ps[0][:, 0:3 * KC], conv_rows[:], ident[0:3 * KC, 0:3 * KC]).then_inc(taps_transposed, 1)

            for unit in range(2 * N_PROJ):
                step, t = divmod(unit, NT)
                if unit < 2:
                    pe.wait_ge(inT_lo_ready, 2 * t + 2)
                else:
                    pe.wait_ge(proj_taken[t], step)
                wide_unit(acc[t], t, 2 * step % SLOTS, 2 * step, done=tile0_done if t == 0 else None)
                if unit in (2, 4):
                    for tile in range(NT):
                        pe.wait_ge(proj_taken[tile], unit // 2)
                        if unit == 4 and tile == 0:
                            pe.wait_ge(head_taken, 1)
                        transpose_cols(q_tok if unit == 2 else k_tok, tile, head_psum)
                head = unit - ATT0
                if 0 <= head < H:
                    if head == 0:
                        pe.wait_ge(head_taken, 2)
                        pe.wait_ge(inT_lo_ready, 4)
                    else:
                        pe.wait_ge(scores_biased, head)
                    part, pair = slice(HD * (head % 2), HD * (head % 2) + HD), head // 2
                    nc.tensor.matmul(score_ps[:, 0:TWO], qT[part, pair, P:TWO], kT[part, pair, :], start=True, stop=True)
                    nc.tensor.matmul(score_ps[:, TWO:ROW], qT[part, pair, 0:P], kT[part, pair, 0:P],
                                     start=True, stop=True).then_inc(scores_ready, 1)
                if 1 <= head <= H:
                    pe.wait_ge(probs_ready, head)
                    if head >= 2:
                        pe.wait_ge(probsT_ready, head - 1)
                    for b in range(3):
                        last = nc.tensor.transpose(probT_ps[:, b * P:(b + 1) * P],
                                                   probs[:, (head - 1) % 2, b * P:(b + 1) * P], ident[:])
                    last.then_inc(probsT_psum, 1)
                if 2 <= head <= H + 1:
                    h = head - 2
                    cols = slice(h * HD, (h + 1) * HD)
                    pe.wait_ge(probsT_ready, h + 1)
                    if h == 0:
                        pe.wait_ge(proj_taken[1], 3)
                        pe.wait_ge(proj_taken[0], 3)
                        pe.wait_ge(taps_ready, 1)
                    nc.tensor.matmul(att_ps[1][:, cols], probsT[:, h % 2, 0:P], v_tok[:, 0, cols], start=True, stop=False)
                    nc.tensor.matmul(att_ps[1][:, cols], probsT[:, h % 2, P:TWO], v_tok[:, 1, cols], start=False, stop=True)
                    nc.tensor.matmul(att_ps[0][:, cols], probsT[:, h % 2, TWO:ROW], v_tok[:, 0, cols],
                                     start=True, stop=True).then_inc(pv_done, 1)
                if unit == 2 * STEP_B:
                    for tile in range(NT):
                        pe.wait_ge(proj_taken[tile], STEP_C + 1)
                        transpose_cols(u_tok, tile, convT_psum)
                if unit == 2 * STEP_B + 2:
                    pe.wait_ge(uT_ready, 1)
                    for tile in range(NT):
                        pe.wait_ge(proj_taken[tile], STEP_B + 1)
                        transpose_cols(gb_tok, tile, convT_psum)
                if unit == ATT0 + H + 3:
                    pe.wait_ge(y_ready, 1)
                    pe.wait_ge(att_ready, 1)
                    for tile in range(NT):
                        transpose_cols(att_tok, tile, attT_psum)
            def branch_unit(t, n):
                for b, (a_hi, a_lo) in enumerate(((midT_hi, midT_lo), (attT_hi, attT_lo))):
                    j = J_BRANCH + 2 * n + b
                    if t == 0:
                        pe.wait_ge(half_lo, j + 1)
                    for k in range(KC):
                        last = product(branch_ps[n][b], a_hi, a_lo, k, t, j % SLOTS, k * W, k == 0, k == KC - 1)
                    if t == 1:
                        last.then_inc(halves_used, 1)
                if t == 0:
                    last.then_inc(branch_done, 1)

            pe.wait_ge(y_lo_ready, 1)
            pe.wait_ge(attT_lo_ready, 2)
            pe.wait_ge(proj_taken[0], N_PROJ)
            pe.wait_ge(proj_taken[1], N_PROJ)
            branch_unit(0, 0)
            pe.wait_ge(probsT_ready, H)
            branch_unit(0, 1)
            pe.wait_ge(gated, 1)
            branch_unit(1, 0)
            pe.wait_ge(m_ready, 2)
            transpose_rows(rows, 0, tr, inT_psum)
            pe.wait_ge(gated, 2)
            branch_unit(1, 1)

            def transpose_m1():
                pe.wait_ge(m_ready, 4)
                pe.wait_ge(inT_lo_ready, 6)
                transpose_rows(rows, 1, tr, inT_psum)

            def transpose_h0():
                pe.wait_ge(h_ready, 1)
                transpose_rows(rows, 0, tr, inT_psum)

            def transpose_h1():
                pe.wait_ge(h_ready, 2)
                pe.wait_ge(inT_lo_ready, 10)
                transpose_rows(rows, 1, tr, inT_psum)

            pe.wait_ge(gated, 3)
            pe.wait_ge(inT_lo_ready, 6)
            wide_unit(mix_ps[0][0], 0, J_O % SLOTS, J_O, done=tile0_done)
            wide_unit(mix_ps[0][1], 0, (J_O + 2) % SLOTS, J_O + 2, done=tile0_done, midway=transpose_m1)
            pe.wait_ge(gated, 4)
            pe.wait_ge(inT_lo_ready, 8)
            wide_unit(mix_ps[1][0], 1, J_O % SLOTS, J_O)
            wide_unit(mix_ps[1][1], 1, (J_O + 2) % SLOTS, J_O + 2, midway=transpose_h0)

            def up_unit(t, bank, slot0, first_half, midway=None):
                wide_unit(bank, t, slot0, first_half, done=tile0_done if t == 0 else None, midway=midway)

            def down_unit(t, slot0, first_half, first=False, last_group=False):
                def part(k, n, stop=False):
                    return product(down_ps[t][n], midT_hi, midT_lo, k, t, slot0 + k // 2, k % 2 * D + n * W,
                                   first and k == 0, stop)

                for h in range(2):
                    if t == 0:
                        pe.wait_ge(half_lo, first_half + h + 1)
                    if last_group:
                        continue
                    for k in (2 * h, 2 * h + 1):
                        for n in range(2):
                            ins = part(k, n)
                    if t == 1:
                        ins.then_inc(halves_used, 1)
                if last_group:
                    for n in range(2):
                        for k in range(KC):
                            ins = part(k, n, stop=k == KC - 1)
                        ins.then_inc(down_done, 1)

            def transpose_hidden(src, t, count):
                pe.wait_ge(hidden_ready, count)
                transpose_cols(src, t, hiddenT_psum)

            pe.wait_ge(inT_lo_ready, 10)
            up_unit(0, acc[0], J_MLP % SLOTS, J_MLP)
            up_unit(0, acc[1], (J_MLP + 2) % SLOTS, J_MLP + 2, midway=transpose_h1)
            pe.wait_ge(inT_lo_ready, 12)
            pe.wait_ge(relu_done, 1)
            up_unit(1, acc[0], J_MLP % SLOTS, J_MLP)
            transpose_hidden(hidden0, 0, 1)
            pe.wait_ge(relu_done, 2)
            up_unit(1, acc[1], (J_MLP + 2) % SLOTS, J_MLP + 2, midway=lambda: transpose_hidden(hidden0, 1, 3))
            pe.wait_ge(hiddenT_lo, 1)
            down_unit(0, 0, J_MLP + 4, first=True)
            transpose_hidden(hidden, 0, 2)
            pe.wait_ge(hiddenT_lo, 2)
            down_unit(1, 0, J_MLP + 4, first=True)
            transpose_hidden(hidden, 1, 4)
            with pe.Fori(0, N_FF - 2) as i:
                for t in range(NT):
                    pe.wait_ge(relu_done, 2 * i + 3 + t)
                    up_unit(t, acc[t], 2, 4 * i + J_MLP + 6)
                for t in range(NT):
                    pe.wait_ge(hiddenT_lo, 2 * i + 3 + t)
                    down_unit(t, 0, 4 * i + J_MLP + 8)
                    transpose_hidden(hidden, t, 2 * i + 5 + t)
            for t in range(NT):
                pe.wait_ge(hiddenT_lo, 2 * N_FF - 1 + t)
                down_unit(t, 2, N_HALVES - 2, last_group=True)


_INS = ["x", "ln_mix_pre", "w_in", "conv_w", "w_conv_out", "w_attn_out", "rel_bias", "w_o",
        "ln_mix_post", "ln_mlp_pre", "w_mlp_in", "w_mlp_out", "ln_mlp_post"]
_OUTS = [((1, 256, 1024), "float32")]


def kernel(**inputs):
    import numpy as _np
    import concourse.bacc as _bacc
    from concourse import mybir as _mybir
    from concourse.bass_utils import run_bass_kernel_spmd as _run

    nc = _bacc.Bacc("TRN2", target_bir_lowering=False, num_devices=1)
    arrays, args = {}, []
    for name in _INS:
        a = _np.ascontiguousarray(inputs[name])
        arrays[f"in_{name}_dram"] = a
        args.append(nc.dram_tensor(f"in_{name}_dram", a.shape, _mybir.dt.from_np(a.dtype), kind="ExternalInput").ap())
    for i, (shape, dtype) in enumerate(_OUTS):
        dt = _mybir.dt.from_np(_np.dtype(dtype))
        args.append(nc.dram_tensor(f"out_{i}_dram", shape, dt, kind="ExternalOutput").ap())
    hybrid_layer(nc, *args)
    r = _run(nc, [arrays], core_ids=[0])
    return r.results[0]["out_0_dram"]
```

```python
from contextlib import ExitStack

import numpy as np

import concourse.bass as bass
from concourse import mybir

F32 = mybir.dt.float32
F32R = mybir.dt.float32r
ACT = mybir.ActivationFunctionType
ALU = mybir.AluOpType

P = 128
EPS = 1e-6
NEG = -1e30
MAX_DISTANCE = 1024


def bucket_runs(seq, n_buckets):
    exact = n_buckets // 2
    n = np.arange(seq)
    far = np.maximum(n, exact).astype(np.float32)
    large = exact + (np.log(far / np.float32(exact)) / np.float32(np.log(MAX_DISTANCE / exact))
                     * np.float32(n_buckets - exact)).astype(np.int32)
    bucket = np.where(n < exact, n, np.minimum(large, n_buckets - 1))
    return [(int(b), int(n[bucket == b][0]), int(n[bucket == b][-1]) + 1) for b in np.unique(bucket)]


def hybrid_layer(nc, x, ln_mix_pre, w_in, conv_w, w_conv_out, w_attn_out, rel_bias, w_o,
                 ln_mix_post, ln_mlp_pre, w_mlp_in, w_mlp_out, ln_mlp_post, out):
    SEQ, D = x.shape[1], x.shape[2]
    H, NBUCKETS = rel_bias.shape
    C = conv_w.shape[2]
    HD = C // H
    D_FF = w_mlp_in.shape[2]
    NT = SEQ // P
    KD, KC = D // P, C // P
    W = 512
    HALF_K = 4
    HALF = HALF_K * W
    SLOTS = 4
    N_PROJ = w_in.shape[2] // W
    N_FF = D_FF // W
    SCALE = float(HD) ** -0.5
    TWO = 2 * P
    ROW = 3 * P
    assert (NT, KD, KC, D // W, C, N_PROJ) == (2, 8, 4, 2, W, 10)

    J_BRANCH = 2 * N_PROJ
    J_O = J_BRANCH + 4
    J_MLP = J_O + 4
    N_HALVES = J_MLP + 4 * N_FF
    XIN, GB, GC, Q, K, V = 0, 1, 2, 3, 4, 5
    ORDER = [Q, K, V, XIN, GC, GB, 6, 7, 8, 9]
    STEP_XIN, STEP_C, STEP_B, STEP_GATES = 3, 4, 5, 6
    ATT0 = 5

    x_v = x.rearrange("b (t p) d -> (b p) t d", p=P)
    out_v = out.rearrange("b (t p) d -> (b p) t d", p=P)
    w_in_v = w_in[0].rearrange("(k p) n -> p k n", p=P)
    w_co_v = w_conv_out[0].rearrange("(k p) n -> p k n", p=P)
    w_ao_v = w_attn_out[0].rearrange("(k p) n -> p k n", p=P)
    w_o_v = w_o[0].rearrange("(k p) n -> p k n", p=P)
    w_up_v = w_mlp_in[0].rearrange("(k p) n -> p k n", p=P)
    w_down_v = w_mlp_out[0].rearrange("(g k p) n -> p g k n", p=P, k=KC)
    bias_rows_dram = nc.dram_tensor("bias_rows_dram", (H, ROW), F32, kind="Internal")

    ctx = ExitStack()
    with ctx:
        def sb(name, shape, dt=F32):
            return ctx.enter_context(nc.sbuf_tensor(name, shape, dt))

        def psum(name):
            return ctx.enter_context(nc.psum_tensor(name, [P, W], F32))

        def sem(name):
            return ctx.enter_context(nc.semaphore(name))

        w_raw = sb("w_raw", [P, SLOTS, HALF])
        w_hi = sb("w_hi", [P, SLOTS, HALF], F32R)
        w_lo = sb("w_lo", [P, SLOTS, HALF], F32R)
        resid = sb("resid", [P, NT, D])
        rows = sb("rows", [P, NT, D])
        inT_hi = sb("inT_hi", [P, KD, SEQ], F32R)
        inT_lo = sb("inT_lo", [P, KD, SEQ], F32R)
        midT_hi = sb("midT_hi", [P, KC, SEQ], F32R)
        midT_lo = sb("midT_lo", [P, KC, SEQ], F32R)
        attT_hi = sb("attT_hi", [P, KC, SEQ], F32R)
        attT_lo = sb("attT_lo", [P, KC, SEQ], F32R)
        gates = sb("gates", [P, NT, 2 * D])
        bufA = sb("bufA", [P, NT, W])
        bufB = sb("bufB", [P, NT, W])
        bufC = sb("bufC", [P, NT, W])
        bufQT = sb("bufQT", [P, KC, SEQ])
        bufKT = sb("bufKT", [P, KC, SEQ])
        bufV = sb("bufV", [P, NT, W])
        q_tok, xin_tok = bufA, bufA
        k_tok, u_tok = bufB, bufB
        conv = bufB[:].rearrange("p t w -> p (t w)").rearrange("p (c s) -> p c s", c=KC)
        gb_tok, att_tok, hidden = bufC, bufC, bufC
        hidden0 = gates[:, :, 0:W]
        squares = gates[:, :, D:2 * D]
        qT, kT, v_tok = bufQT, bufKT, bufV
        g_post = bufQT[:].rearrange("p c s -> p (c s)")
        g_mlp = bufKT[:].rearrange("p c s -> p (c s)")
        g_last = bufV[:].rearrange("p t w -> p (t w)")
        uT = sb("uT", [P, KC, 2 + SEQ])
        bias = sb("bias", [P, H, TWO])
        probs = sb("probs", [P, 2, 3 * P])
        probsT = sb("probsT", [P, 2, 3 * P])
        bias_row = gates[0:H, 0, 0:ROW]
        bias_tab = gates[0:H, 0, W - 2 * NBUCKETS:W]
        vec_rows = gates[0:KD + 3 * KC, 1, 0:P]
        vec_cols = sb("vec_cols", [P, KD + 3 * KC])
        ident = sb("ident", [P, P])
        neg_max = sb("neg_max", [P, NT, H])
        den = sb("den", [P, NT, H])
        rden = sb("rden", [P, NT, H])
        ss = sb("ss", [P, 16])
        var = sb("var", [P, 8])
        std = sb("std", [P, 8])
        newton = sb("newton", [P, 8])
        inv0 = sb("inv0", [P, 8])
        inv = sb("inv", [P, 8])

        acc = [psum("acc0"), psum("acc1")]
        score_ps = psum("score_ps")
        probT_ps = psum("probT_ps")
        att_ps = [psum("att0"), psum("att1")]
        tr = [psum("tr0"), psum("tr1")]
        xT_ps = [tr[0], tr[1], score_ps, probT_ps]
        branch_ps = [(score_ps, probT_ps), (acc[0], acc[1])]
        mix_ps = [(score_ps, probT_ps), (acc[0], acc[1])]
        down_ps = [(att_ps[0], att_ps[1]), (score_ps, probT_ps)]

        x_loaded = [sem(f"x_loaded{t}") for t in range(NT)]
        gain_loaded = sem("gain_loaded")
        conv_w_loaded = sem("conv_w_loaded")
        piece_loaded = [sem(f"piece_loaded{i}") for i in range(4)]
        rel_bias_loaded = sem("rel_bias_loaded")
        half_loaded = [sem(f"half_loaded{s}") for s in range(SLOTS)]
        bias_rows_stored = sem("bias_rows_stored")
        bias_loaded = sem("bias_loaded")
        gains_loaded = [sem(f"gains_loaded{i}") for i in range(3)]
        stored = sem("stored")
        pool_seq = sem("pool_seq")
        consts_ready = sem("consts_ready")
        bias_row_ready = sem("bias_row_ready")
        piece_hi = sem("piece_hi")
        piece_lo = sem("piece_lo")
        half_hi = sem("half_hi")
        half_lo = sem("half_lo")
        halves_used = sem("halves_used")
        dve_seq = sem("dve_seq")
        vecs_psum = sem("vecs_psum")
        vecs_ready = sem("vecs_ready")
        xT_psum = sem("xT_psum")
        xT_hi = sem("xT_hi")
        xT_lo = sem("xT_lo")
        squared = sem("squared")
        var_ready = sem("var_ready")
        std_ready = sem("std_ready")
        inv_ready = sem("inv_ready")
        inT_psum = sem("inT_psum")
        inT_hi_ready = sem("inT_hi_ready")
        inT_lo_ready = sem("inT_lo_ready")
        tile0_done = sem("tile0_done")
        proj_taken = [sem(f"proj_taken{t}") for t in range(NT)]
        head_psum = sem("head_psum")
        head_taken = sem("head_taken")
        scores_ready = sem("scores_ready")
        scores_biased = sem("scores_biased")
        probs_ready = sem("probs_ready")
        probsT_psum = sem("probsT_psum")
        probsT_ready = sem("probsT_ready")
        pv_done = sem("pv_done")
        att_ready = sem("att_ready")
        convT_psum = sem("convT_psum")
        uT_ready = sem("uT_ready")
        y_ready = sem("y_ready")
        y_hi_ready = sem("y_hi_ready")
        y_lo_ready = sem("y_lo_ready")
        attT_psum = sem("attT_psum")
        attT_hi_ready = sem("attT_hi_ready")
        attT_lo_ready = sem("attT_lo_ready")
        branch_done = sem("branch_done")
        gated = sem("gated")
        m_ready = sem("m_ready")
        mix_gained = sem("mix_gained")
        resid_ready = sem("resid_ready")
        h_ready = sem("h_ready")
        relu_done = sem("relu_done")
        hidden_ready = sem("hidden_ready")
        hiddenT_psum = sem("hiddenT_psum")
        hiddenT_hi = sem("hiddenT_hi")
        hiddenT_lo = sem("hiddenT_lo")
        down_done = sem("down_done")
        down_gained = sem("down_gained")
        out_ready = sem("out_ready")

        MIX_SQUARED = ((3, 4), (5, 7))
        RESID_SQUARED = (6, 8)

        def half_landed(j, slot):
            return 16 * (j // SLOTS + (slot >= 2))

        block = ctx.enter_context(nc.Block())

        @block.sync
        def _(sp):
            def load_half(j, slot, src, cols=W):
                if not isinstance(j, int) or j >= SLOTS:
                    sp.wait_ge(half_lo, j - (SLOTS - 1))
                sp.dma_start(w_raw[:, slot, :].rearrange("p (k n) -> p k n", n=cols), src).then_inc(
                    half_loaded[slot], 16)

            def load_square_half(j, w_v, n, h):
                load_half(j, j % SLOTS, w_v[:, h * HALF_K:(h + 1) * HALF_K, n * W:(n + 1) * W])

            sp.dma_start(vec_rows[0:KD, :], ln_mix_pre.rearrange("o (k p) -> (o k) p", p=P)).then_inc(gain_loaded, 16)
            sp.dma_start(resid[:, 0, :], x_v[:, 0, :]).then_inc(x_loaded[0], 16)
            sp.dma_start(vec_rows[KD:KD + 3 * KC, :], conv_w[0].rearrange("j (c p) -> (j c) p", p=P)).then_inc(
                conv_w_loaded, 16)
            for i in range(4):
                sp.dma_start(w_raw[:, i // 2, i % 2 * D:(i % 2 + 1) * D].rearrange("p (k n) -> p k n", n=W),
                             w_in_v[:, 2 * i:2 * i + 2, ORDER[0] * W:(ORDER[0] + 1) * W]).then_inc(piece_loaded[i], 16)
            sp.dma_start(resid[:, 1, :], x_v[:, 1, :]).then_inc(x_loaded[1], 16)
            sp.dma_start(bias_tab[:, 0:NBUCKETS], rel_bias).then_inc(rel_bias_loaded, 16)
            for j in range(2, 8):
                load_square_half(j, w_in_v, ORDER[j // 2], j % 2)
            sp.wait_ge(bias_row_ready, 1)
            sp.dma_start(bias_rows_dram.ap(), bias_row[:]).then_inc(bias_rows_stored, 16)
            sp.wait_ge(bias_rows_stored, 16)
            sp.dma_start(bias[:], bass.AP(tensor=bias_rows_dram, offset=0,
                                          ap=[[1, P], [ROW, H], [1, TWO]])).then_inc(bias_loaded, 16)
            for j in range(8, J_BRANCH):
                load_square_half(j, w_in_v, ORDER[j // 2], j % 2)
            for n in range(2):
                load_square_half(J_BRANCH + 2 * n, w_co_v, n, 0)
                load_square_half(J_BRANCH + 2 * n + 1, w_ao_v, n, 0)
            sp.wait_ge(pv_done, H)
            for i, (dst, gain) in enumerate(((g_post, ln_mix_post), (g_mlp, ln_mlp_pre), (g_last, ln_mlp_post))):
                sp.dma_start(dst, gain[0].partition_broadcast(P)).then_inc(gains_loaded[i], 16)
            for n in range(2):
                for h in range(2):
                    load_square_half(J_O + 2 * n + h, w_o_v, n, h)
            for g in range(2):
                for h in range(2):
                    load_square_half(J_MLP + 2 * g + h, w_up_v, g, h)

            def load_down(j, g, slot0):
                for h in range(2):
                    src = w_down_v[:, bass.ts(g, 1), 2 * h:2 * h + 2, :].rearrange("p g k n -> p (g k) n")
                    load_half(j + h, slot0 + h, src, cols=D)

            def load_up(j, g, slot0):
                for h in range(2):
                    load_half(j + h, slot0 + h, w_up_v[:, h * HALF_K:(h + 1) * HALF_K, bass.ts(g, W)])

            load_down(J_MLP + 4, 0, 0)
            load_up(J_MLP + 6, 2, 2)
            with sp.Fori(0, N_FF - 3) as i:
                load_down(4 * i + J_MLP + 8, i + 1, 0)
                load_up(4 * i + J_MLP + 10, i + 3, 2)
            load_down(N_HALVES - 4, N_FF - 2, 0)
            load_down(N_HALVES - 2, N_FF - 1, 2)
            for t in range(NT):
                for n in range(2):
                    sp.wait_ge(out_ready, 2 * t + n + 1)
                    sp.dma_start(out_v[:, t, n * W:(n + 1) * W], rows[:, t, n * W:(n + 1) * W]).then_inc(stored, 16)
            sp.wait_ge(stored, 16 * 2 * NT)

        @block.gpsimd
        def _(pool):
            seq = [0]

            def link(ins):
                seq[0] += 1
                ins.then_inc(pool_seq, 1)
                pool.wait_ge(pool_seq, seq[0])

            link(nc.gpsimd.memset(ident[:], 0.0))
            nc.gpsimd.affine_select(out=ident[:], in_=ident[:], compare_op=ALU.not_equal, fill=1.0, base=0,
                                    pattern=[[-1, P]], channel_multiplier=1).then_inc(consts_ready, 1)
            nc.gpsimd.memset(uT[:, :, 0:2], 0.0).then_inc(consts_ready, 1)
            link(nc.gpsimd.memset(bias_row[:], NEG / SCALE))
            pool.wait_ge(rel_bias_loaded, 16)
            link(nc.gpsimd.tensor_scalar(bias_tab[:, NBUCKETS:], bias_tab[:, 0:NBUCKETS], 1.0 / SCALE, 1.0,
                                         ALU.mult, ALU.mult))
            for b, lo, hi in bucket_runs(SEQ, NBUCKETS):
                last = nc.gpsimd.tensor_copy(bias_row[:, P - 1 + lo:P - 1 + hi],
                                             bias_tab[:, NBUCKETS + b:NBUCKETS + b + 1].to_broadcast([H, hi - lo]))
            last.then_inc(bias_row_ready, 1)
            for t in range(NT):
                for n in range(2):
                    pool.wait_ge(gated, 2 * t + n + 1)
                    cols = slice(n * W, (n + 1) * W)
                    nc.gpsimd.tensor_tensor(rows[:, t, cols], gates[:, t, cols], gates[:, t, D + n * W:D + (n + 1) * W],
                                            ALU.add).then_inc(m_ready, 1)
            j = J_MLP + 3
            pool.wait_ge(half_hi, j - 1)
            pool.wait_ge(half_lo, j)
            nc.gpsimd.tensor_tensor(w_lo[:, j % SLOTS, :], w_raw[:, j % SLOTS, :], w_hi[:, j % SLOTS, :].bitcast(F32),
                                    ALU.subtract).then_inc(half_lo, 1)

        @block.scalar
        def _(act):
            def split_hi(j, slot, used):
                act.wait_ge(half_loaded[slot], used)
                if not isinstance(j, int) or j >= SLOTS:
                    act.wait_ge(halves_used, j - (SLOTS - 1))
                nc.scalar.copy(w_hi[:, slot, :], w_raw[:, slot, :]).then_inc(half_hi, 1)

            def split_half(j):
                split_hi(j, j % SLOTS, half_landed(j, j % SLOTS))

            def inT_hi_tile(t, count):
                act.wait_ge(inT_psum, count)
                for b in range(2):
                    nc.scalar.copy(inT_hi[:, 4 * b:4 * b + 4, t * P:(t + 1) * P],
                                   tr[b][:].rearrange("p (k s) -> p k s", s=P)).then_inc(inT_hi_ready, 1)

            def xT_hi_bank(t, b):
                act.wait_ge(xT_psum, 4 * t + b + 1)
                for k in (2 * b, 2 * b + 1):
                    ins = nc.scalar.activation(inT_hi[:, k, t * P:(t + 1) * P], xT_ps[b][:, k % 2 * P:(k % 2 + 1) * P],
                                               ACT.Copy, scale=vec_cols[:, k:k + 1])
                ins.then_inc(xT_hi, 1)

            def split_piece(i):
                act.wait_ge(piece_loaded[i], 16)
                cols = slice(i % 2 * D, (i % 2 + 1) * D)
                nc.scalar.copy(w_hi[:, i // 2, cols], w_raw[:, i // 2, cols]).then_inc(piece_hi, 1)

            def root(col, count, width=1):
                act.wait_ge(var_ready, count)
                nc.scalar.activation(std[:, col:col + width], var[:, col:col + width], ACT.Sqrt).then_inc(std_ready, 1)

            def x_squares(t):
                act.wait_ge(x_loaded[t], 16)
                nc.scalar.activation(squares[:, t, :], resid[:, t, :], ACT.Square,
                                     accum_out=ss[:, t:t + 1]).then_inc(squared, 1)

            nc.scalar.preload_act_table(ACT.Sqrt)
            act.wait_ge(vecs_ready, 1)
            xT_hi_bank(0, 0)
            split_piece(0)
            xT_hi_bank(0, 1)
            split_piece(1)
            xT_hi_bank(0, 2)
            xT_hi_bank(0, 3)
            split_piece(2)
            split_piece(3)
            x_squares(0)
            for b in range(4):
                xT_hi_bank(1, b)
            split_half(2)
            x_squares(1)
            root(0, 1, NT)
            split_half(3)
            act.wait_ge(inv_ready, 1)

            for unit in range(2 * N_PROJ):
                step, t = divmod(unit, NT)
                if t == 1:
                    split_half(2 * step + 4)
                head = unit - ATT0
                if 0 <= head < H:
                    act.wait_ge(scores_biased, head + 1)
                    for tile, cols in ((1, slice(0, TWO)), (0, slice(TWO, ROW))):
                        ins = nc.scalar.activation(probs[:, head % 2, cols], probs[:, head % 2, cols], ACT.Exp,
                                                   bias=neg_max[:, tile, head:head + 1], scale=-1.0,
                                                   accum_out=den[:, tile, head:head + 1])
                    ins.then_inc(probs_ready, 1)
                if step != STEP_C:
                    if t == 0:
                        act.wait_ge(tile0_done, step + 1)
                    else:
                        act.wait_ge(halves_used, 2 * step + 2)
                    rms = inv[:, t:t + 1]
                    if step >= STEP_GATES:
                        g = step - STEP_GATES
                        nc.scalar.activation(gates[:, t, g * W:(g + 1) * W], acc[t][:], ACT.Sigmoid,
                                             scale=rms).then_inc(proj_taken[t], 1)
                    else:
                        if step == STEP_XIN:
                            act.wait_ge(head_psum, 2)
                        dst = {0: q_tok, 1: k_tok, 2: v_tok, STEP_XIN: xin_tok, STEP_B: gb_tok}[step]
                        nc.scalar.activation(dst[:, t, :], acc[t][:], ACT.Copy, scale=rms).then_inc(proj_taken[t], 1)
                if unit == 2 * STEP_B + 3:
                    act.wait_ge(y_ready, 1)
                    nc.scalar.copy(midT_hi[:], conv).then_inc(y_hi_ready, 1)
                if unit == ATT0 + H + 3:
                    for tile in range(NT):
                        act.wait_ge(attT_psum, tile + 1)
                        nc.scalar.copy(attT_hi[:, :, tile * P:(tile + 1) * P],
                                       tr[tile][:].rearrange("p (k s) -> p k s", s=P)).then_inc(attT_hi_ready, 1)
                if t == 1:
                    split_half(2 * step + 5)

            nc.scalar.preload_act_table(ACT.Sqrt)
            split_half(J_O)
            inT_hi_tile(0, 1)
            for j in range(J_O + 1, J_O + 4):
                split_half(j)
            inT_hi_tile(1, 2)

            def square_sum(src, dst, col):
                nc.scalar.activation(dst, src, ACT.Square, accum_out=ss[:, col:col + 1]).then_inc(squared, 1)

            def mix_squares(t, n):
                if t == 0:
                    act.wait_ge(tile0_done, N_PROJ + n + 1)
                else:
                    act.wait_ge(halves_used, J_O + 2 * n + 2)
                square_sum(mix_ps[t][n][:], squares[:, t, n * W:(n + 1) * W], 2 + 2 * t + n)

            def resid_squares(t):
                act.wait_ge(resid_ready, t + 1)
                square_sum(resid[:, t, :], squares[:, t, :], 6 + t)

            mix_squares(0, 0)
            mix_squares(0, 1)
            root(2, 2)
            split_half(J_MLP)
            inT_hi_tile(0, 3)
            mix_squares(1, 0)
            split_half(J_MLP + 1)
            resid_squares(0)
            split_half(J_MLP + 2)
            mix_squares(1, 1)
            root(4, 3)
            split_half(J_MLP + 3)
            root(3, 4)

            def relu_squared(bank, dst, t, count):
                nc.scalar.activation(dst, bank[:], ACT.Relu, scale=inv[:, 4 + t:5 + t]).then_inc(relu_done, 1)
                act.wait_ge(relu_done, count)
                nc.scalar.activation(dst, dst, ACT.Square).then_inc(hidden_ready, 1)

            def hiddenT_hi_tile(t, count):
                act.wait_ge(hiddenT_psum, count)
                nc.scalar.copy(midT_hi[:, :, t * P:(t + 1) * P],
                               tr[t][:].rearrange("p (k s) -> p k s", s=P)).then_inc(hiddenT_hi, 1)

            act.wait_ge(inv_ready, 3)
            act.wait_ge(tile0_done, N_PROJ + 3)
            relu_squared(score_ps, hidden0[:, 0, :], 0, 1)
            resid_squares(1)
            inT_hi_tile(1, 4)
            root(5, 5)
            act.wait_ge(tile0_done, N_PROJ + 4)
            relu_squared(probT_ps, hidden[:, 0, :], 0, 2)
            act.wait_ge(inv_ready, 5)
            act.wait_ge(halves_used, J_MLP + 2)
            relu_squared(acc[0], hidden0[:, 1, :], 1, 3)
            hiddenT_hi_tile(0, 1)
            split_half(J_MLP + 4)
            hiddenT_hi_tile(1, 2)
            split_half(J_MLP + 5)
            act.wait_ge(halves_used, J_MLP + 4)
            relu_squared(acc[1], hidden[:, 1, :], 1, 4)
            split_half(J_MLP + 6)
            split_half(J_MLP + 7)
            hiddenT_hi_tile(0, 3)
            hiddenT_hi_tile(1, 4)
            with act.Fori(0, N_FF - 2) as i:
                for h in range(2):
                    split_hi(4 * i + J_MLP + 8 + h, h, 16 * i + half_landed(J_MLP + 8, h))
                act.wait_ge(tile0_done, i + N_PROJ + 5)
                relu_squared(acc[0], hidden[:, 0, :], 0, 2 * i + 5)
                act.wait_ge(halves_used, 4 * i + J_MLP + 8)
                relu_squared(acc[1], hidden[:, 1, :], 1, 2 * i + 6)
                for h in range(2):
                    split_hi(4 * i + J_MLP + 10 + h, 2 + h, 16 * i + half_landed(J_MLP + 10, 2 + h))
                hiddenT_hi_tile(0, 2 * i + 5)
                hiddenT_hi_tile(1, 2 * i + 6)
            for t in range(NT):
                for n in range(2):
                    act.wait_ge(down_done, 2 * t + n + 1)
                    square_sum(down_ps[t][n][:], squares[:, t, n * W:(n + 1) * W], 8 + 2 * t + n)
                root(6 + t, 6 + t)

        @block.vector
        def _(dve):
            seq = [0]

            def link(ins):
                seq[0] += 1
                ins.then_inc(dve_seq, 1)
                dve.wait_ge(dve_seq, seq[0])

            def split_lo(j, slot):
                dve.wait_ge(half_hi, j - 1)
                nc.vector.tensor_tensor(w_lo[:, slot, :], w_raw[:, slot, :], w_hi[:, slot, :].bitcast(F32),
                                        ALU.subtract).then_inc(half_lo, 1)

            def split_half(j):
                split_lo(j, j % SLOTS)

            def xT_lo_bank(t, b):
                dve.wait_ge(xT_hi, 4 * t + b + 1)
                for k in (2 * b, 2 * b + 1):
                    cols = slice(t * P, (t + 1) * P)
                    ins = nc.vector.scalar_tensor_tensor(out=inT_lo[:, k, cols], in0=xT_ps[b][:, k % 2 * P:(k % 2 + 1) * P],
                                                         scalar=vec_cols[:, k:k + 1], in1=inT_hi[:, k, cols].bitcast(F32),
                                                         op0=ALU.mult, op1=ALU.subtract)
                ins.then_inc(xT_lo, 1)

            def split_piece(i):
                dve.wait_ge(piece_hi, i + 1)
                cols = slice(i % 2 * D, (i % 2 + 1) * D)
                nc.vector.tensor_tensor(w_lo[:, i // 2, cols], w_raw[:, i // 2, cols], w_hi[:, i // 2, cols].bitcast(F32),
                                        ALU.subtract).then_inc(half_lo if i % 2 else piece_lo, 1)

            def inT_lo_tile(t, count):
                for b in range(2):
                    dve.wait_ge(inT_hi_ready, 2 * count - 1 + b)
                    nc.vector.tensor_tensor(inT_lo[:, 4 * b:4 * b + 4, t * P:(t + 1) * P],
                                            tr[b][:].rearrange("p (k s) -> p k s", s=P),
                                            inT_hi[:, 4 * b:4 * b + 4, t * P:(t + 1) * P].bitcast(F32),
                                            ALU.subtract).then_inc(inT_lo_ready, 1)

            def mean_square(dst, sums, count, plus):
                dve.wait_ge(squared, count)
                if isinstance(plus, float):
                    return nc.vector.tensor_scalar(dst, sums, 1.0 / D, plus, ALU.mult, ALU.add)
                return nc.vector.scalar_tensor_tensor(out=dst, in0=sums, scalar=1.0 / D, in1=plus,
                                                      op0=ALU.mult, op1=ALU.add)

            def inverse(col, width, count):
                s = slice(col, col + width)
                dve.wait_ge(std_ready, count)
                link(nc.vector.reciprocal(inv0[:, s], std[:, s]))
                for c in range(col, col + width):
                    ins = nc.vector.scalar_tensor_tensor(out=newton[:, c:c + 1], in0=inv0[:, c:c + 1], scalar=inv0[:, c:c + 1],
                                                         in1=var[:, c:c + 1], op0=ALU.mult, op1=ALU.mult)
                link(ins)
                link(nc.vector.tensor_scalar(newton[:, s], newton[:, s], -0.5, 1.5, ALU.mult, ALU.add))
                nc.vector.tensor_tensor(inv[:, s], inv0[:, s], newton[:, s], ALU.mult).then_inc(inv_ready, 1)
                dve.wait_ge(inv_ready, count)

            dve.wait_ge(vecs_psum, 1)
            nc.vector.tensor_copy(vec_cols[:], att_ps[0][:, 0:KD + 3 * KC]).then_inc(vecs_ready, 1)
            dve.wait_ge(vecs_ready, 1)
            xT_lo_bank(0, 0)
            split_piece(0)
            xT_lo_bank(0, 1)
            split_piece(1)
            xT_lo_bank(0, 2)
            xT_lo_bank(0, 3)
            split_piece(2)
            split_piece(3)
            for b in range(4):
                xT_lo_bank(1, b)
            split_half(2)
            mean_square(var[:, 0:NT], ss[:, 0:NT], 2, EPS).then_inc(var_ready, 1)
            inverse(0, NT, 1)
            split_half(3)

            def tap(j, c):
                return vec_cols[:, KD + j * KC + c:KD + j * KC + c + 1]

            for unit in range(2 * N_PROJ):
                step, t = divmod(unit, NT)
                if t == 1:
                    split_half(2 * step + 4)
                head = unit - ATT0
                if unit in (2, 4):
                    dve.wait_ge(head_psum, unit)
                    for tile in range(NT):
                        ins = nc.vector.tensor_copy((qT if unit == 2 else kT)[:, :, tile * P:(tile + 1) * P],
                                                    tr[tile][:].rearrange("p (k s) -> p k s", s=P))
                    ins.then_inc(head_taken, 1)
                if 0 <= head < H:
                    if head == 0:
                        dve.wait_ge(bias_loaded, 16)
                    dve.wait_ge(scores_ready, head + 1)
                    if head >= 2:
                        dve.wait_ge(probsT_psum, head - 1)
                    for tile, cols, window in ((1, slice(0, TWO), slice(TWO - 1, None, -1)),
                                               (0, slice(TWO, ROW), slice(P - 1, None, -1))):
                        ins = nc.vector.tensor_tensor_reduce(
                            out=probs[:, head % 2, cols], in0=score_ps[:, cols], in1=bias[:, head, window],
                            scale=-SCALE, scalar=3.0e38, op0=ALU.add, op1=ALU.min,
                            accum_out=neg_max[:, tile, head:head + 1])
                    ins.then_inc(scores_biased, 1)
                if 1 <= head <= H:
                    dve.wait_ge(probsT_psum, head)
                    if head >= 3:
                        dve.wait_ge(pv_done, head - 2)
                    nc.vector.tensor_copy(probsT[:, (head - 1) % 2, :], probT_ps[:, 0:ROW]).then_inc(probsT_ready, 1)
                if step == STEP_C:
                    if t == 0:
                        dve.wait_ge(tile0_done, step + 1)
                        dve.wait_ge(head_psum, 4)
                    else:
                        dve.wait_ge(halves_used, 2 * step + 2)
                    dve.wait_ge(proj_taken[t], STEP_XIN + 1)
                    nc.vector.scalar_tensor_tensor(out=u_tok[:, t, :], in0=acc[t][:], scalar=inv[:, t:t + 1],
                                                   in1=xin_tok[:, t, :], op0=ALU.mult, op1=ALU.mult).then_inc(
                                                       proj_taken[t], 1)
                if unit == 2 * STEP_B:
                    dve.wait_ge(convT_psum, 2)
                    for tile in range(NT):
                        ins = nc.vector.tensor_copy(uT[:, :, 2 + tile * P:2 + (tile + 1) * P],
                                                    tr[tile][:].rearrange("p (k s) -> p k s", s=P))
                    ins.then_inc(uT_ready, 1)
                    dve.wait_ge(uT_ready, 1)
                if unit == 2 * STEP_B + 1:
                    for c in range(KC):
                        ins = nc.vector.tensor_scalar(conv[:, c, :], uT[:, c, 2:2 + SEQ], tap(2, c), None, ALU.mult)
                    link(ins)
                    for j in (1, 0):
                        for c in range(KC):
                            ins = nc.vector.scalar_tensor_tensor(out=conv[:, c, :], in0=uT[:, c, j:j + SEQ],
                                                                 scalar=tap(j, c), in1=conv[:, c, :],
                                                                 op0=ALU.mult, op1=ALU.add)
                        link(ins)
                if unit == 2 * STEP_B + 3:
                    dve.wait_ge(convT_psum, 4)
                    for tile in range(NT):
                        half_conv = conv[:, :, tile * P:(tile + 1) * P]
                        ins = nc.vector.tensor_tensor(half_conv, tr[tile][:].rearrange("p (k s) -> p k s", s=P),
                                                      half_conv, ALU.mult)
                    ins.then_inc(y_ready, 1)
                    dve.wait_ge(y_hi_ready, 1)
                    nc.vector.tensor_tensor(midT_lo[:], conv, midT_hi[:].bitcast(F32), ALU.subtract).then_inc(y_lo_ready, 1)
                if unit == ATT0 + H + 2:
                    link(nc.vector.reciprocal(rden[:], den[:]))
                    dve.wait_ge(pv_done, H)
                    for tile in range(NT):
                        ins = nc.vector.tensor_tensor(att_tok[:, tile, :].rearrange("p (h d) -> p h d", h=H),
                                                      att_ps[tile][:].rearrange("p (h d) -> p h d", h=H),
                                                      rden[:, tile, :].unsqueeze(2).to_broadcast([P, H, HD]), ALU.mult)
                    ins.then_inc(att_ready, 1)
                if unit == ATT0 + H + 3:
                    for tile in range(NT):
                        cols = slice(tile * P, (tile + 1) * P)
                        dve.wait_ge(attT_hi_ready, tile + 1)
                        nc.vector.tensor_tensor(attT_lo[:, :, cols], tr[tile][:].rearrange("p (k s) -> p k s", s=P),
                                                attT_hi[:, :, cols].bitcast(F32), ALU.subtract).then_inc(attT_lo_ready, 1)
                if t == 1:
                    split_half(2 * step + 5)

            def gate(t, n):
                if t == 0:
                    dve.wait_ge(branch_done, n + 1)
                else:
                    dve.wait_ge(halves_used, J_BRANCH + 2 * n + 2)
                for b in range(2):
                    g = gates[:, t, b * D + n * W:b * D + (n + 1) * W]
                    ins = nc.vector.tensor_tensor(g, branch_ps[n][b][:], g, ALU.mult)
                ins.then_inc(gated, 1)

            gate(0, 0)
            gate(0, 1)
            split_half(J_O)
            gate(1, 0)
            inT_lo_tile(0, 1)
            split_half(J_O + 1)
            gate(1, 1)
            split_half(J_O + 2)
            split_half(J_O + 3)
            inT_lo_tile(1, 2)

            def mix_gain(t, n):
                dve.wait_ge(squared, MIX_SQUARED[t][n])
                cols = slice(n * W, (n + 1) * W)
                nc.vector.tensor_tensor(rows[:, t, cols], mix_ps[t][n][:], g_post[:, cols], ALU.mult).then_inc(mix_gained, 1)

            def residual(t):
                dve.wait_ge(mix_gained, 2 * t + 2)
                nc.vector.scalar_tensor_tensor(out=resid[:, t, :], in0=rows[:, t, :], scalar=inv[:, 2 + t:3 + t],
                                               in1=resid[:, t, :], op0=ALU.mult, op1=ALU.add).then_inc(resid_ready, 1)
                dve.wait_ge(resid_ready, t + 1)
                nc.vector.tensor_tensor(rows[:, t, :], resid[:, t, :], g_mlp, ALU.mult).then_inc(h_ready, 1)

            dve.wait_ge(gains_loaded[0], 16)
            dve.wait_ge(gains_loaded[1], 16)
            def mix_variance(t, n):
                if n == 0:
                    link(mean_square(var[:, 2 + t:3 + t], ss[:, 2 + 2 * t:3 + 2 * t], MIX_SQUARED[t][n], EPS))
                else:
                    mean_square(var[:, 2 + t:3 + t], ss[:, 3 + 2 * t:4 + 2 * t], MIX_SQUARED[t][n],
                                var[:, 2 + t:3 + t]).then_inc(var_ready, 1)

            mix_gain(0, 0)
            mix_variance(0, 0)
            mix_variance(0, 1)
            mix_gain(0, 1)
            inverse(2, 1, 2)
            residual(0)
            split_half(J_MLP)
            inT_lo_tile(0, 3)
            mix_gain(1, 0)
            mix_variance(1, 0)
            split_half(J_MLP + 1)
            mean_square(var[:, 4:5], ss[:, 6:7], RESID_SQUARED[0], EPS).then_inc(var_ready, 1)
            split_half(J_MLP + 2)
            mix_variance(1, 1)
            mix_gain(1, 1)
            inverse(4, 1, 3)
            inverse(3, 1, 4)
            residual(1)
            mean_square(var[:, 5:6], ss[:, 7:8], RESID_SQUARED[1], EPS).then_inc(var_ready, 1)
            inT_lo_tile(1, 4)
            inverse(5, 1, 5)

            def hiddenT_lo_tile(t, count):
                dve.wait_ge(hiddenT_hi, count)
                nc.vector.tensor_tensor(midT_lo[:, :, t * P:(t + 1) * P], tr[t][:].rearrange("p (k s) -> p k s", s=P),
                                        midT_hi[:, :, t * P:(t + 1) * P].bitcast(F32),
                                        ALU.subtract).then_inc(hiddenT_lo, 1)

            hiddenT_lo_tile(0, 1)
            split_half(J_MLP + 4)
            hiddenT_lo_tile(1, 2)
            split_half(J_MLP + 5)
            split_half(J_MLP + 6)
            split_half(J_MLP + 7)
            hiddenT_lo_tile(0, 3)
            hiddenT_lo_tile(1, 4)
            with dve.Fori(0, N_FF - 2) as i:
                for h in range(4):
                    split_lo(4 * i + J_MLP + 8 + h, h)
                hiddenT_lo_tile(0, 2 * i + 5)
                hiddenT_lo_tile(1, 2 * i + 6)
            dve.wait_ge(gains_loaded[2], 16)
            for t in range(NT):
                for n in range(2):
                    cols = slice(n * W, (n + 1) * W)
                    v, part = var[:, 6 + t:7 + t], ss[:, 8 + 2 * t + n:9 + 2 * t + n]
                    if n == 0:
                        link(mean_square(v, part, 9 + 2 * t, EPS))
                    else:
                        mean_square(v, part, 10 + 2 * t, v).then_inc(var_ready, 1)
                    nc.vector.tensor_tensor(rows[:, t, cols], down_ps[t][n][:], g_last[:, cols],
                                            ALU.mult).then_inc(down_gained, 1)
                inverse(6 + t, 1, 6 + t)
                dve.wait_ge(down_gained, 2 * t + 2)
                for n in range(2):
                    cols = slice(n * W, (n + 1) * W)
                    nc.vector.scalar_tensor_tensor(out=rows[:, t, cols], in0=rows[:, t, cols], scalar=inv[:, 6 + t:7 + t],
                                                   in1=resid[:, t, cols], op0=ALU.mult, op1=ALU.add).then_inc(out_ready, 1)

        @block.tensor
        def _(pe):
            def product(bank, a_hi, a_lo, k, t, slot, off, start, stop):
                hi, lo = a_hi[:, k, t * P:(t + 1) * P], a_lo[:, k, t * P:(t + 1) * P]
                b_hi, b_lo = w_hi[:, slot, off:off + W], w_lo[:, slot, off:off + W]
                nc.tensor.matmul(bank[:], hi, b_hi, start=start, stop=False)
                nc.tensor.matmul(bank[:], hi, b_lo, start=False, stop=False)
                return nc.tensor.matmul(bank[:], lo, b_hi, start=False, stop=stop)

            def wide_unit(bank, t, slot0, first_half, done=None, midway=None, before=None):
                for k in range(KD):
                    if before is not None:
                        before(k)
                    elif t == 0 and k % HALF_K == 0:
                        pe.wait_ge(half_lo, first_half + k // HALF_K + 1)
                    if k == HALF_K and midway is not None:
                        midway()
                    last = product(bank, inT_hi, inT_lo, k, t, slot0 + k // HALF_K, k % HALF_K * W, k == 0, k == KD - 1)
                    if t == 1 and k % HALF_K == HALF_K - 1 and (done is None or k < KD - 1):
                        last.then_inc(halves_used, 1)
                if done is not None:
                    last.then_inc(done, 1)

            def transpose_rows(src, t, done):
                for k in range(KD):
                    last = nc.tensor.transpose(tr[k // 4][:, k % 4 * P:(k % 4 + 1) * P],
                                               src[:, t, k * P:(k + 1) * P], ident[:])
                last.then_inc(done, 1)

            def transpose_cols(src, t, done):
                for k in range(KC):
                    last = nc.tensor.transpose(tr[t][:, k * P:(k + 1) * P], src[:, t, k * P:(k + 1) * P], ident[:])
                last.then_inc(done, 1)

            def transpose_x(t):
                for k in range(KD):
                    last = nc.tensor.transpose(xT_ps[k // 2][:, k % 2 * P:(k % 2 + 1) * P],
                                               resid[:, t, k * P:(k + 1) * P], ident[:])
                    if k % 2:
                        last.then_inc(xT_psum, 1)

            pe.wait_ge(consts_ready, 1)
            pe.wait_ge(gain_loaded, 16)
            pe.wait_ge(conv_w_loaded, 16)
            nc.tensor.transpose(att_ps[0][:, 0:KD + 3 * KC], vec_rows[:],
                                ident[0:KD + 3 * KC, 0:KD + 3 * KC]).then_inc(vecs_psum, 1)
            pe.wait_ge(x_loaded[0], 16)
            transpose_x(0)

            def before_first(k):
                if k == HALF_K:
                    pe.wait_ge(x_loaded[1], 16)
                    pe.wait_ge(xT_lo, 4)
                    transpose_x(1)
                if k % 2 == 0:
                    pe.wait_ge(xT_lo, k // 2 + 1)
                    pe.wait_ge(half_lo if k % 4 else piece_lo, k // 4 + 1)

            def before_second(k):
                if k % 2 == 0:
                    pe.wait_ge(xT_lo, 4 + k // 2 + 1)

            for unit in range(2 * N_PROJ):
                step, t = divmod(unit, NT)
                if unit >= 2:
                    pe.wait_ge(proj_taken[t], step)
                wide_unit(acc[t], t, 2 * step % SLOTS, 2 * step, done=tile0_done if t == 0 else None,
                          before={0: before_first, 1: before_second}.get(unit))
                if unit in (2, 4):
                    for tile in range(NT):
                        pe.wait_ge(proj_taken[tile], unit // 2)
                        if unit == 4 and tile == 0:
                            pe.wait_ge(head_taken, 1)
                        transpose_cols(q_tok if unit == 2 else k_tok, tile, head_psum)
                head = unit - ATT0
                if 0 <= head < H:
                    if head == 0:
                        pe.wait_ge(head_taken, 2)
                    else:
                        pe.wait_ge(scores_biased, head)
                    part, pair = slice(HD * (head % 2), HD * (head % 2) + HD), head // 2
                    nc.tensor.matmul(score_ps[:, 0:TWO], qT[part, pair, P:TWO], kT[part, pair, :], start=True, stop=True)
                    nc.tensor.matmul(score_ps[:, TWO:ROW], qT[part, pair, 0:P], kT[part, pair, 0:P],
                                     start=True, stop=True).then_inc(scores_ready, 1)
                if 1 <= head <= H:
                    pe.wait_ge(probs_ready, head)
                    if head >= 2:
                        pe.wait_ge(probsT_ready, head - 1)
                    for b in range(3):
                        last = nc.tensor.transpose(probT_ps[:, b * P:(b + 1) * P],
                                                   probs[:, (head - 1) % 2, b * P:(b + 1) * P], ident[:])
                    last.then_inc(probsT_psum, 1)
                if 2 <= head <= H + 1:
                    h = head - 2
                    cols = slice(h * HD, (h + 1) * HD)
                    pe.wait_ge(probsT_ready, h + 1)
                    if h == 0:
                        pe.wait_ge(proj_taken[1], 3)
                        pe.wait_ge(proj_taken[0], 3)
                    nc.tensor.matmul(att_ps[1][:, cols], probsT[:, h % 2, 0:P], v_tok[:, 0, cols], start=True, stop=False)
                    nc.tensor.matmul(att_ps[1][:, cols], probsT[:, h % 2, P:TWO], v_tok[:, 1, cols], start=False, stop=True)
                    nc.tensor.matmul(att_ps[0][:, cols], probsT[:, h % 2, TWO:ROW], v_tok[:, 0, cols],
                                     start=True, stop=True).then_inc(pv_done, 1)
                if unit == 2 * STEP_B:
                    for tile in range(NT):
                        pe.wait_ge(proj_taken[tile], STEP_C + 1)
                        transpose_cols(u_tok, tile, convT_psum)
                if unit == 2 * STEP_B + 2:
                    pe.wait_ge(uT_ready, 1)
                    for tile in range(NT):
                        pe.wait_ge(proj_taken[tile], STEP_B + 1)
                        transpose_cols(gb_tok, tile, convT_psum)
                if unit == ATT0 + H + 3:
                    pe.wait_ge(y_ready, 1)
                    pe.wait_ge(att_ready, 1)
                    for tile in range(NT):
                        transpose_cols(att_tok, tile, attT_psum)
            def branch_unit(t, n):
                for b, (a_hi, a_lo) in enumerate(((midT_hi, midT_lo), (attT_hi, attT_lo))):
                    j = J_BRANCH + 2 * n + b
                    if t == 0:
                        pe.wait_ge(half_lo, j + 1)
                    for k in range(KC):
                        last = product(branch_ps[n][b], a_hi, a_lo, k, t, j % SLOTS, k * W, k == 0, k == KC - 1)
                    if t == 1:
                        last.then_inc(halves_used, 1)
                if t == 0:
                    last.then_inc(branch_done, 1)

            pe.wait_ge(y_lo_ready, 1)
            pe.wait_ge(attT_lo_ready, 2)
            pe.wait_ge(probsT_ready, H)
            branch_unit(0, 0)
            pe.wait_ge(proj_taken[0], N_PROJ)
            pe.wait_ge(proj_taken[1], N_PROJ)
            branch_unit(0, 1)
            pe.wait_ge(gated, 1)
            branch_unit(1, 0)
            pe.wait_ge(m_ready, 2)
            transpose_rows(rows, 0, inT_psum)
            pe.wait_ge(gated, 2)
            branch_unit(1, 1)

            def transpose_m1():
                pe.wait_ge(m_ready, 4)
                pe.wait_ge(inT_lo_ready, 2)
                transpose_rows(rows, 1, inT_psum)

            def transpose_h0():
                pe.wait_ge(h_ready, 1)
                transpose_rows(rows, 0, inT_psum)

            def transpose_h1():
                pe.wait_ge(h_ready, 2)
                transpose_rows(rows, 1, inT_psum)

            pe.wait_ge(gated, 3)
            pe.wait_ge(inT_lo_ready, 2)
            wide_unit(mix_ps[0][0], 0, J_O % SLOTS, J_O, done=tile0_done)
            wide_unit(mix_ps[0][1], 0, (J_O + 2) % SLOTS, J_O + 2, done=tile0_done, midway=transpose_m1)
            pe.wait_ge(gated, 4)
            pe.wait_ge(inT_lo_ready, 4)
            wide_unit(mix_ps[1][0], 1, J_O % SLOTS, J_O)
            transpose_h0()
            wide_unit(mix_ps[1][1], 1, (J_O + 2) % SLOTS, J_O + 2)

            def up_unit(t, bank, slot0, first_half, midway=None):
                wide_unit(bank, t, slot0, first_half, done=tile0_done if t == 0 else None, midway=midway)

            def down_unit(t, slot0, first_half, first=False, last_group=False):
                def part(k, n, stop=False):
                    return product(down_ps[t][n], midT_hi, midT_lo, k, t, slot0 + k // 2, k % 2 * D + n * W,
                                   first and k == 0, stop)

                for h in range(2):
                    if t == 0:
                        pe.wait_ge(half_lo, first_half + h + 1)
                    if last_group:
                        continue
                    for k in (2 * h, 2 * h + 1):
                        for n in range(2):
                            ins = part(k, n)
                    if t == 1:
                        ins.then_inc(halves_used, 1)
                if last_group:
                    for n in range(2):
                        for k in range(KC):
                            ins = part(k, n, stop=k == KC - 1)
                        ins.then_inc(down_done, 1)

            def transpose_hidden(src, t, count):
                pe.wait_ge(hidden_ready, count)
                transpose_cols(src, t, hiddenT_psum)

            pe.wait_ge(inT_lo_ready, 6)
            up_unit(0, score_ps, J_MLP % SLOTS, J_MLP)
            up_unit(0, probT_ps, (J_MLP + 2) % SLOTS, J_MLP + 2, midway=transpose_h1)
            pe.wait_ge(inT_lo_ready, 8)
            up_unit(1, acc[0], J_MLP % SLOTS, J_MLP)
            transpose_hidden(hidden0, 0, 1)
            up_unit(1, acc[1], (J_MLP + 2) % SLOTS, J_MLP + 2, midway=lambda: transpose_hidden(hidden0, 1, 3))
            pe.wait_ge(hiddenT_lo, 1)
            down_unit(0, 0, J_MLP + 4, first=True)
            transpose_hidden(hidden, 0, 2)
            pe.wait_ge(hiddenT_lo, 2)
            pe.wait_ge(relu_done, 2)
            down_unit(1, 0, J_MLP + 4, first=True)
            transpose_hidden(hidden, 1, 4)
            with pe.Fori(0, N_FF - 2) as i:
                for t in range(NT):
                    pe.wait_ge(relu_done, 2 * i + 3 + t)
                    up_unit(t, acc[t], 2, 4 * i + J_MLP + 6)
                for t in range(NT):
                    pe.wait_ge(hiddenT_lo, 2 * i + 3 + t)
                    down_unit(t, 0, 4 * i + J_MLP + 8)
                    transpose_hidden(hidden, t, 2 * i + 5 + t)
            for t in range(NT):
                pe.wait_ge(hiddenT_lo, 2 * N_FF - 1 + t)
                down_unit(t, 2, N_HALVES - 2, last_group=True)


_INS = ["x", "ln_mix_pre", "w_in", "conv_w", "w_conv_out", "w_attn_out", "rel_bias", "w_o",
        "ln_mix_post", "ln_mlp_pre", "w_mlp_in", "w_mlp_out", "ln_mlp_post"]
_OUTS = [((1, 256, 1024), "float32")]


def kernel(**inputs):
    import numpy as _np
    import concourse.bacc as _bacc
    from concourse import mybir as _mybir
    from concourse.bass_utils import run_bass_kernel_spmd as _run

    nc = _bacc.Bacc("TRN2", target_bir_lowering=False, num_devices=1)
    arrays, args = {}, []
    for name in _INS:
        a = _np.ascontiguousarray(inputs[name])
        arrays[f"in_{name}_dram"] = a
        args.append(nc.dram_tensor(f"in_{name}_dram", a.shape, _mybir.dt.from_np(a.dtype), kind="ExternalInput").ap())
    for i, (shape, dtype) in enumerate(_OUTS):
        dt = _mybir.dt.from_np(_np.dtype(dtype))
        args.append(nc.dram_tensor(f"out_{i}_dram", shape, dt, kind="ExternalOutput").ap())
    hybrid_layer(nc, *args)
    r = _run(nc, [arrays], core_ids=[0])
    return r.results[0]["out_0_dram"]
```

```python
from contextlib import ExitStack

import numpy as np

import concourse.bass as bass
from concourse import mybir

F32 = mybir.dt.float32
F32R = mybir.dt.float32r
ACT = mybir.ActivationFunctionType
ALU = mybir.AluOpType

P = 128
EPS = 1e-6
NEG = -1e30
MAX_DISTANCE = 1024


def bucket_runs(seq, n_buckets):
    exact = n_buckets // 2
    n = np.arange(seq)
    far = np.maximum(n, exact).astype(np.float32)
    large = exact + (np.log(far / np.float32(exact)) / np.float32(np.log(MAX_DISTANCE / exact))
                     * np.float32(n_buckets - exact)).astype(np.int32)
    bucket = np.where(n < exact, n, np.minimum(large, n_buckets - 1))
    return [(int(b), int(n[bucket == b][0]), int(n[bucket == b][-1]) + 1) for b in np.unique(bucket)]


def hybrid_layer(nc, x, ln_mix_pre, w_in, conv_w, w_conv_out, w_attn_out, rel_bias, w_o,
                 ln_mix_post, ln_mlp_pre, w_mlp_in, w_mlp_out, ln_mlp_post, out):
    SEQ, D = x.shape[1], x.shape[2]
    H, NBUCKETS = rel_bias.shape
    C = conv_w.shape[2]
    HD = C // H
    D_FF = w_mlp_in.shape[2]
    NT = SEQ // P
    KD, KC = D // P, C // P
    W = 512
    HALF_K = 4
    HALF = HALF_K * W
    SLOTS = 4
    N_PROJ = w_in.shape[2] // W
    N_FF = D_FF // W
    SCALE = float(HD) ** -0.5
    TWO = 2 * P
    ROW = 3 * P
    assert (NT, KD, KC, D // W, C, N_PROJ) == (2, 8, 4, 2, W, 10)

    J_BRANCH = 2 * N_PROJ
    J_O = J_BRANCH + 4
    J_MLP = J_O + 4
    N_HALVES = J_MLP + 4 * N_FF
    XIN, GB, GC, Q, K, V = 0, 1, 2, 3, 4, 5
    ORDER = [Q, K, V, XIN, GC, GB, 6, 7, 8, 9]
    STEP_XIN, STEP_C, STEP_B, STEP_GATES = 3, 4, 5, 6
    ATT0 = 5

    x_v = x.rearrange("b (t p) d -> (b p) t d", p=P)
    out_v = out.rearrange("b (t p) d -> (b p) t d", p=P)
    w_in_v = w_in[0].rearrange("(k p) n -> p k n", p=P)
    w_co_v = w_conv_out[0].rearrange("(k p) n -> p k n", p=P)
    w_ao_v = w_attn_out[0].rearrange("(k p) n -> p k n", p=P)
    w_o_v = w_o[0].rearrange("(k p) n -> p k n", p=P)
    w_up_v = w_mlp_in[0].rearrange("(k p) n -> p k n", p=P)
    w_down_v = w_mlp_out[0].rearrange("(g k p) n -> p g k n", p=P, k=KC)
    bias_rows_dram = nc.dram_tensor("bias_rows_dram", (H, ROW), F32, kind="Internal")

    ctx = ExitStack()
    with ctx:
        def sb(name, shape, dt=F32):
            return ctx.enter_context(nc.sbuf_tensor(name, shape, dt))

        def psum(name):
            return ctx.enter_context(nc.psum_tensor(name, [P, W], F32))

        def sem(name):
            return ctx.enter_context(nc.semaphore(name))

        w_raw = sb("w_raw", [P, SLOTS, HALF])
        w_hi = sb("w_hi", [P, SLOTS, HALF], F32R)
        w_lo = sb("w_lo", [P, SLOTS, HALF], F32R)
        resid = sb("resid", [P, NT, D])
        rows = sb("rows", [P, NT, D])
        inT_hi = sb("inT_hi", [P, KD, SEQ], F32R)
        inT_lo = sb("inT_lo", [P, KD, SEQ], F32R)
        midT_hi = sb("midT_hi", [P, KC, SEQ], F32R)
        midT_lo = sb("midT_lo", [P, KC, SEQ], F32R)
        attT_hi = sb("attT_hi", [P, KC, SEQ], F32R)
        attT_lo = sb("attT_lo", [P, KC, SEQ], F32R)
        gates = sb("gates", [P, NT, 2 * D])
        bufA = sb("bufA", [P, NT, W])
        bufB = sb("bufB", [P, NT, W])
        bufC = sb("bufC", [P, NT, W])
        bufQT = sb("bufQT", [P, KC, SEQ])
        bufKT = sb("bufKT", [P, KC, SEQ])
        bufV = sb("bufV", [P, NT, W])
        q_tok, xin_tok = bufA, bufA
        k_tok, u_tok = bufB, bufB
        conv = bufB[:].rearrange("p t w -> p (t w)").rearrange("p (c s) -> p c s", c=KC)
        gb_tok, att_tok, hidden = bufC, bufC, bufC
        hidden0 = gates[:, :, 0:W]
        squares = gates[:, :, D:2 * D]
        qT, kT, v_tok = bufQT, bufKT, bufV
        g_post = bufQT[:].rearrange("p c s -> p (c s)")
        g_mlp = bufKT[:].rearrange("p c s -> p (c s)")
        g_last = bufV[:].rearrange("p t w -> p (t w)")
        uT = sb("uT", [P, KC, 2 + SEQ])
        bias = sb("bias", [P, H, TWO])
        probs = sb("probs", [P, 2, 3 * P])
        probsT = sb("probsT", [P, 2, 3 * P])
        bias_row = gates[0:H, 0, 0:ROW]
        bias_tab = gates[0:H, 0, W - 2 * NBUCKETS:W]
        gain_rows = gates[0:KD, 1, 0:P]
        tap_rows = gates[0:3 * KC, 1, P:2 * P]
        gain_cols = sb("gain_cols", [P, KD])
        tap_cols = sb("tap_cols", [P, 3 * KC])
        ident = sb("ident", [P, P])
        neg_max = sb("neg_max", [P, NT, H])
        den = sb("den", [P, NT, H])
        rden = sb("rden", [P, NT, H])
        ss = sb("ss", [P, 16])
        var = sb("var", [P, 8])
        std = sb("std", [P, 8])
        newton = sb("newton", [P, 8])
        inv0 = sb("inv0", [P, 8])
        inv = sb("inv", [P, 8])

        acc = [psum("acc0"), psum("acc1")]
        score_ps = psum("score_ps")
        probT_ps = psum("probT_ps")
        att_ps = [psum("att0"), psum("att1")]
        tr = [psum("tr0"), psum("tr1")]
        xT_ps = [tr[0], tr[1], score_ps, probT_ps]
        proj_ps = [att_ps, acc, att_ps] + [acc] * (N_PROJ - 3)
        branch_ps = [(score_ps, probT_ps), (acc[0], acc[1])]
        mix_ps = [(score_ps, probT_ps), (acc[0], acc[1])]
        down_ps = [(att_ps[0], att_ps[1]), (score_ps, probT_ps)]

        x_loaded = [sem(f"x_loaded{i}") for i in range(KD // 2)]
        gain_loaded = sem("gain_loaded")
        taps_loaded = sem("taps_loaded")
        piece_loaded = [sem(f"piece_loaded{i}") for i in range(KD)]
        rel_bias_loaded = sem("rel_bias_loaded")
        half_loaded = [sem(f"half_loaded{s}") for s in range(SLOTS)]
        bias_rows_stored = sem("bias_rows_stored")
        bias_loaded = sem("bias_loaded")
        gains_loaded = [sem(f"gains_loaded{i}") for i in range(3)]
        stored = sem("stored")
        pool_seq = sem("pool_seq")
        consts_ready = sem("consts_ready")
        bias_row_ready = sem("bias_row_ready")
        piece_hi = sem("piece_hi")
        piece_lo = sem("piece_lo")
        half_hi = sem("half_hi")
        half_lo = sem("half_lo")
        early_lo = sem("early_lo")
        halves_used = sem("halves_used")
        dve_seq = sem("dve_seq")
        gain_psum = sem("gain_psum")
        gain_ready = sem("gain_ready")
        taps_psum = sem("taps_psum")
        taps_ready = sem("taps_ready")
        xT_psum = sem("xT_psum")
        xT_hi = sem("xT_hi")
        xT_lo = sem("xT_lo")
        squared = sem("squared")
        var_ready = sem("var_ready")
        std_ready = sem("std_ready")
        inv_ready = sem("inv_ready")
        inT_psum = sem("inT_psum")
        inT_hi_ready = sem("inT_hi_ready")
        inT_lo_ready = sem("inT_lo_ready")
        tile0_done = sem("tile0_done")
        proj_taken = [sem(f"proj_taken{t}") for t in range(NT)]
        head_psum = sem("head_psum")
        head_taken = sem("head_taken")
        scores_ready = sem("scores_ready")
        scores_biased = sem("scores_biased")
        probs_ready = sem("probs_ready")
        probsT_psum = sem("probsT_psum")
        probsT_ready = sem("probsT_ready")
        pv_done = sem("pv_done")
        att_ready = sem("att_ready")
        convT_psum = sem("convT_psum")
        uT_ready = sem("uT_ready")
        y_ready = sem("y_ready")
        y_hi_ready = sem("y_hi_ready")
        y_lo_ready = sem("y_lo_ready")
        attT_psum = sem("attT_psum")
        attT_hi_ready = sem("attT_hi_ready")
        attT_lo_ready = sem("attT_lo_ready")
        branch_done = sem("branch_done")
        gated = sem("gated")
        m_ready = sem("m_ready")
        mix_gained = sem("mix_gained")
        resid_ready = sem("resid_ready")
        h_ready = sem("h_ready")
        relu_done = sem("relu_done")
        hidden_ready = sem("hidden_ready")
        hiddenT_psum = sem("hiddenT_psum")
        hiddenT_hi = sem("hiddenT_hi")
        hiddenT_lo = sem("hiddenT_lo")
        down_done = sem("down_done")
        down_gained = sem("down_gained")
        out_ready = sem("out_ready")

        MIX_SQUARED = ((3, 4), (5, 7))
        RESID_SQUARED = (6, 8)

        def half_landed(j, slot):
            return 16 * (j // SLOTS + (slot >= 2))

        block = ctx.enter_context(nc.Block())

        @block.sync
        def _(sp):
            def load_half(j, slot, src, cols=W):
                if not isinstance(j, int) or j >= SLOTS:
                    sp.wait_ge(half_lo, j - (SLOTS - 1))
                sp.dma_start(w_raw[:, slot, :].rearrange("p (k n) -> p k n", n=cols), src).then_inc(
                    half_loaded[slot], 16)

            def load_square_half(j, w_v, n, h):
                load_half(j, j % SLOTS, w_v[:, h * HALF_K:(h + 1) * HALF_K, n * W:(n + 1) * W])

            for i in range(KD // 2):
                cols = slice(2 * i * P, 2 * (i + 1) * P)
                sp.dma_start(resid[:, :, cols], x_v[:, :, cols]).then_inc(x_loaded[i], 16)
                for k in (2 * i, 2 * i + 1):
                    sp.dma_start(w_raw[:, k // HALF_K, k % HALF_K * W:(k % HALF_K + 1) * W],
                                 w_in_v[:, k, ORDER[0] * W:(ORDER[0] + 1) * W]).then_inc(piece_loaded[k], 16)
            sp.dma_start(tap_rows, conv_w[0].rearrange("j (c p) -> (j c) p", p=P)).then_inc(taps_loaded, 16)
            sp.dma_start(bias_tab[:, 0:NBUCKETS], rel_bias).then_inc(rel_bias_loaded, 16)
            for j in range(2, 8):
                load_square_half(j, w_in_v, ORDER[j // 2], j % 2)
            sp.wait_ge(bias_row_ready, 1)
            sp.dma_start(bias_rows_dram.ap(), bias_row[:]).then_inc(bias_rows_stored, 16)
            sp.wait_ge(bias_rows_stored, 16)
            sp.dma_start(bias[:], bass.AP(tensor=bias_rows_dram, offset=0,
                                          ap=[[1, P], [ROW, H], [1, TWO]])).then_inc(bias_loaded, 16)
            for j in range(8, J_BRANCH):
                load_square_half(j, w_in_v, ORDER[j // 2], j % 2)
            for n in range(2):
                load_square_half(J_BRANCH + 2 * n, w_co_v, n, 0)
                load_square_half(J_BRANCH + 2 * n + 1, w_ao_v, n, 0)
            sp.wait_ge(pv_done, H)
            for i, (dst, gain) in enumerate(((g_post, ln_mix_post), (g_mlp, ln_mlp_pre), (g_last, ln_mlp_post))):
                sp.dma_start(dst, gain[0].partition_broadcast(P)).then_inc(gains_loaded[i], 16)
            for n in range(2):
                for h in range(2):
                    load_square_half(J_O + 2 * n + h, w_o_v, n, h)
            for g in range(2):
                for h in range(2):
                    load_square_half(J_MLP + 2 * g + h, w_up_v, g, h)

            def load_down(j, g, slot0):
                for h in range(2):
                    src = w_down_v[:, bass.ts(g, 1), 2 * h:2 * h + 2, :].rearrange("p g k n -> p (g k) n")
                    load_half(j + h, slot0 + h, src, cols=D)

            def load_up(j, g, slot0):
                for h in range(2):
                    load_half(j + h, slot0 + h, w_up_v[:, h * HALF_K:(h + 1) * HALF_K, bass.ts(g, W)])

            load_down(J_MLP + 4, 0, 0)
            load_up(J_MLP + 6, 2, 2)
            with sp.Fori(0, N_FF - 3) as i:
                load_down(4 * i + J_MLP + 8, i + 1, 0)
                load_up(4 * i + J_MLP + 10, i + 3, 2)
            load_down(N_HALVES - 4, N_FF - 2, 0)
            load_down(N_HALVES - 2, N_FF - 1, 2)
            for t in range(NT):
                for n in range(2):
                    sp.wait_ge(out_ready, 2 * t + n + 1)
                    sp.dma_start(out_v[:, t, n * W:(n + 1) * W], rows[:, t, n * W:(n + 1) * W]).then_inc(stored, 16)
            sp.wait_ge(stored, 16 * 2 * NT)

        @block.gpsimd
        def _(pool):
            seq = [0]

            def link(ins):
                seq[0] += 1
                ins.then_inc(pool_seq, 1)
                pool.wait_ge(pool_seq, seq[0])

            link(nc.gpsimd.memset(ident[:], 0.0))
            nc.gpsimd.affine_select(out=ident[:], in_=ident[:], compare_op=ALU.not_equal, fill=1.0, base=0,
                                    pattern=[[-1, P]], channel_multiplier=1).then_inc(consts_ready, 1)
            nc.gpsimd.memset(uT[:, :, 0:2], 0.0).then_inc(consts_ready, 1)
            link(nc.gpsimd.memset(bias_row[:], NEG / SCALE))
            pool.wait_ge(rel_bias_loaded, 16)
            link(nc.gpsimd.tensor_scalar(bias_tab[:, NBUCKETS:], bias_tab[:, 0:NBUCKETS], 1.0 / SCALE, 1.0,
                                         ALU.mult, ALU.mult))
            for b, lo, hi in bucket_runs(SEQ, NBUCKETS):
                last = nc.gpsimd.tensor_copy(bias_row[:, P - 1 + lo:P - 1 + hi],
                                             bias_tab[:, NBUCKETS + b:NBUCKETS + b + 1].to_broadcast([H, hi - lo]))
            last.then_inc(bias_row_ready, 1)
            for t in range(NT):
                for n in range(2):
                    pool.wait_ge(gated, 2 * t + n + 1)
                    cols = slice(n * W, (n + 1) * W)
                    nc.gpsimd.tensor_tensor(rows[:, t, cols], gates[:, t, cols], gates[:, t, D + n * W:D + (n + 1) * W],
                                            ALU.add).then_inc(m_ready, 1)
            j = J_MLP + 3
            pool.wait_ge(half_hi, j - 1)
            pool.wait_ge(half_lo, j)
            for part, done in ((slice(0, HALF // 2), early_lo), (slice(HALF // 2, HALF), half_lo)):
                nc.gpsimd.tensor_tensor(w_lo[:, j % SLOTS, part], w_raw[:, j % SLOTS, part],
                                        w_hi[:, j % SLOTS, part].bitcast(F32), ALU.subtract).then_inc(done, 1)

        @block.scalar
        def _(act):
            def split_hi(j, slot, used):
                act.wait_ge(half_loaded[slot], used)
                if not isinstance(j, int) or j >= SLOTS:
                    act.wait_ge(halves_used, j - (SLOTS - 1))
                nc.scalar.copy(w_hi[:, slot, :], w_raw[:, slot, :]).then_inc(half_hi, 1)

            def split_half(j):
                split_hi(j, j % SLOTS, half_landed(j, j % SLOTS))

            def inT_hi_tile(t, count):
                act.wait_ge(inT_psum, count)
                for b in range(2):
                    nc.scalar.copy(inT_hi[:, 4 * b:4 * b + 4, t * P:(t + 1) * P],
                                   tr[b][:].rearrange("p (k s) -> p k s", s=P)).then_inc(inT_hi_ready, 1)

            def xT_hi_block(k):
                act.wait_ge(xT_psum, k + 1)
                nc.scalar.activation(inT_hi[:, k, :], xT_ps[k % 4][:, 0:SEQ], ACT.Copy,
                                     scale=gain_cols[:, k:k + 1]).then_inc(xT_hi, 1)

            def split_piece(k):
                act.wait_ge(piece_loaded[k], 16)
                cols = slice(k % HALF_K * W, (k % HALF_K + 1) * W)
                nc.scalar.copy(w_hi[:, k // HALF_K, cols], w_raw[:, k // HALF_K, cols]).then_inc(piece_hi, 1)

            def root(col, count, width=1):
                act.wait_ge(var_ready, count)
                nc.scalar.activation(std[:, col:col + width], var[:, col:col + width], ACT.Sqrt).then_inc(std_ready, 1)

            def x_squares(t):
                nc.scalar.activation(squares[:, t, :], resid[:, t, :], ACT.Square,
                                     accum_out=ss[:, t:t + 1]).then_inc(squared, 1)

            def rms_scaled(t, dst, step):
                nc.scalar.activation(dst[:, t, :], proj_ps[step][t][:], ACT.Copy,
                                     scale=inv[:, t:t + 1]).then_inc(proj_taken[t], 1)

            act.dma_start(gain_rows, ln_mix_pre.rearrange("o (k p) -> (o k) p", p=P)).then_inc(gain_loaded, 16)
            nc.scalar.preload_act_table(ACT.Sqrt)
            act.wait_ge(gain_ready, 1)
            for k in range(KD):
                if k == KD - 3:
                    for loaded in x_loaded:
                        act.wait_ge(loaded, 16)
                    x_squares(0)
                if k == KD - 2:
                    x_squares(1)
                xT_hi_block(k)
                split_piece(k)
            root(0, 1, NT)
            split_half(2)
            split_half(3)
            act.wait_ge(inv_ready, 1)
            act.wait_ge(tile0_done, 1)
            rms_scaled(0, q_tok, 0)
            act.wait_ge(halves_used, 2)
            rms_scaled(1, q_tok, 0)
            for j in (4, 5, 6):
                split_half(j)
            act.wait_ge(tile0_done, 2)
            rms_scaled(0, k_tok, 1)
            act.wait_ge(halves_used, 4)
            rms_scaled(1, k_tok, 1)
            split_half(7)

            for unit in range(4, 2 * N_PROJ):
                step, t = divmod(unit, NT)
                if t == 1:
                    split_half(2 * step + 4)
                head = unit - ATT0
                if 0 <= head < H:
                    act.wait_ge(scores_biased, head + 1)
                    for tile, cols in ((1, slice(0, TWO)), (0, slice(TWO, ROW))):
                        ins = nc.scalar.activation(probs[:, head % 2, cols], probs[:, head % 2, cols], ACT.Exp,
                                                   bias=neg_max[:, tile, head:head + 1], scale=-1.0,
                                                   accum_out=den[:, tile, head:head + 1])
                    ins.then_inc(probs_ready, 1)
                if step != STEP_C:
                    if t == 0:
                        act.wait_ge(tile0_done, step + 1)
                    else:
                        act.wait_ge(halves_used, 2 * step + 2)
                    if step >= STEP_GATES:
                        g = step - STEP_GATES
                        nc.scalar.activation(gates[:, t, g * W:(g + 1) * W], proj_ps[step][t][:], ACT.Sigmoid,
                                             scale=inv[:, t:t + 1]).then_inc(proj_taken[t], 1)
                    else:
                        if step == STEP_XIN:
                            act.wait_ge(head_psum, 2)
                        rms_scaled(t, {2: v_tok, STEP_XIN: xin_tok, STEP_B: gb_tok}[step], step)
                if unit == 2 * STEP_B + 3:
                    act.wait_ge(y_ready, 1)
                    nc.scalar.copy(midT_hi[:], conv).then_inc(y_hi_ready, 1)
                if unit == ATT0 + H + 3:
                    for tile in range(NT):
                        act.wait_ge(attT_psum, tile + 1)
                        nc.scalar.copy(attT_hi[:, :, tile * P:(tile + 1) * P],
                                       tr[tile][:].rearrange("p (k s) -> p k s", s=P)).then_inc(attT_hi_ready, 1)
                if t == 1:
                    split_half(2 * step + 5)

            nc.scalar.preload_act_table(ACT.Sqrt)
            split_half(J_O)
            inT_hi_tile(0, 1)
            for j in range(J_O + 1, J_O + 4):
                split_half(j)
            inT_hi_tile(1, 2)

            def square_sum(src, dst, col):
                nc.scalar.activation(dst, src, ACT.Square, accum_out=ss[:, col:col + 1]).then_inc(squared, 1)

            def mix_squares(t, n):
                if t == 0:
                    act.wait_ge(tile0_done, N_PROJ + n + 1)
                else:
                    act.wait_ge(halves_used, J_O + 2 * n + 2)
                square_sum(mix_ps[t][n][:], squares[:, t, n * W:(n + 1) * W], 2 + 2 * t + n)

            def resid_squares(t):
                act.wait_ge(resid_ready, t + 1)
                square_sum(resid[:, t, :], squares[:, t, :], 6 + t)

            mix_squares(0, 0)
            mix_squares(0, 1)
            root(2, 2)
            split_half(J_MLP)
            inT_hi_tile(0, 3)
            mix_squares(1, 0)
            split_half(J_MLP + 1)
            resid_squares(0)
            split_half(J_MLP + 2)
            mix_squares(1, 1)
            root(4, 3)
            split_half(J_MLP + 3)
            root(3, 4)

            def relu_squared(bank, dst, t, count):
                nc.scalar.activation(dst, bank[:], ACT.Relu, scale=inv[:, 4 + t:5 + t]).then_inc(relu_done, 1)
                act.wait_ge(relu_done, count)
                nc.scalar.activation(dst, dst, ACT.Square).then_inc(hidden_ready, 1)

            def hiddenT_hi_tile(t, count):
                act.wait_ge(hiddenT_psum, count)
                nc.scalar.copy(midT_hi[:, :, t * P:(t + 1) * P],
                               tr[t][:].rearrange("p (k s) -> p k s", s=P)).then_inc(hiddenT_hi, 1)

            act.wait_ge(inv_ready, 3)
            act.wait_ge(tile0_done, N_PROJ + 3)
            relu_squared(score_ps, hidden0[:, 0, :], 0, 1)
            resid_squares(1)
            inT_hi_tile(1, 4)
            root(5, 5)
            act.wait_ge(tile0_done, N_PROJ + 4)
            relu_squared(probT_ps, hidden[:, 0, :], 0, 2)
            split_half(J_MLP + 4)
            act.wait_ge(inv_ready, 5)
            act.wait_ge(halves_used, J_MLP + 2)
            relu_squared(acc[0], hidden0[:, 1, :], 1, 3)
            hiddenT_hi_tile(0, 1)
            split_half(J_MLP + 5)
            hiddenT_hi_tile(1, 2)
            split_half(J_MLP + 6)
            act.wait_ge(halves_used, J_MLP + 4)
            relu_squared(acc[1], hidden[:, 1, :], 1, 4)
            split_half(J_MLP + 7)
            hiddenT_hi_tile(0, 3)
            hiddenT_hi_tile(1, 4)
            with act.Fori(0, N_FF - 2) as i:
                for h in range(2):
                    split_hi(4 * i + J_MLP + 8 + h, h, 16 * i + half_landed(J_MLP + 8, h))
                act.wait_ge(tile0_done, i + N_PROJ + 5)
                relu_squared(acc[0], hidden[:, 0, :], 0, 2 * i + 5)
                act.wait_ge(halves_used, 4 * i + J_MLP + 8)
                relu_squared(acc[1], hidden[:, 1, :], 1, 2 * i + 6)
                for h in range(2):
                    split_hi(4 * i + J_MLP + 10 + h, 2 + h, 16 * i + half_landed(J_MLP + 10, 2 + h))
                hiddenT_hi_tile(0, 2 * i + 5)
                hiddenT_hi_tile(1, 2 * i + 6)
            for t in range(NT):
                for n in range(2):
                    act.wait_ge(down_done, 2 * t + n + 1)
                    square_sum(down_ps[t][n][:], squares[:, t, n * W:(n + 1) * W], 8 + 2 * t + n)
                root(6 + t, 6 + t)

        @block.vector
        def _(dve):
            seq = [0]

            def link(ins):
                seq[0] += 1
                ins.then_inc(dve_seq, 1)
                dve.wait_ge(dve_seq, seq[0])

            def split_lo(j, slot):
                dve.wait_ge(half_hi, j - 1)
                nc.vector.tensor_tensor(w_lo[:, slot, :], w_raw[:, slot, :], w_hi[:, slot, :].bitcast(F32),
                                        ALU.subtract).then_inc(half_lo, 1)

            def split_half(j):
                split_lo(j, j % SLOTS)

            def xT_lo_block(k):
                dve.wait_ge(xT_hi, k + 1)
                nc.vector.scalar_tensor_tensor(out=inT_lo[:, k, :], in0=xT_ps[k % 4][:, 0:SEQ],
                                               scalar=gain_cols[:, k:k + 1], in1=inT_hi[:, k, :].bitcast(F32),
                                               op0=ALU.mult, op1=ALU.subtract).then_inc(xT_lo, 1)

            def split_piece(k):
                dve.wait_ge(piece_hi, k + 1)
                slot, cols = k // HALF_K, slice(k % HALF_K * W, (k % HALF_K + 1) * W)
                nc.vector.tensor_tensor(w_lo[:, slot, cols], w_raw[:, slot, cols], w_hi[:, slot, cols].bitcast(F32),
                                        ALU.subtract).then_inc(half_lo if k % HALF_K == HALF_K - 1 else piece_lo, 1)

            def inT_lo_tile(t, count):
                for b in range(2):
                    dve.wait_ge(inT_hi_ready, 2 * count - 1 + b)
                    nc.vector.tensor_tensor(inT_lo[:, 4 * b:4 * b + 4, t * P:(t + 1) * P],
                                            tr[b][:].rearrange("p (k s) -> p k s", s=P),
                                            inT_hi[:, 4 * b:4 * b + 4, t * P:(t + 1) * P].bitcast(F32),
                                            ALU.subtract).then_inc(inT_lo_ready, 1)

            def mean_square(dst, sums, count, plus):
                dve.wait_ge(squared, count)
                if isinstance(plus, float):
                    return nc.vector.tensor_scalar(dst, sums, 1.0 / D, plus, ALU.mult, ALU.add)
                return nc.vector.scalar_tensor_tensor(out=dst, in0=sums, scalar=1.0 / D, in1=plus,
                                                      op0=ALU.mult, op1=ALU.add)

            def inverse(col, width, count):
                s = slice(col, col + width)
                dve.wait_ge(std_ready, count)
                link(nc.vector.reciprocal(inv0[:, s], std[:, s]))
                for c in range(col, col + width):
                    ins = nc.vector.scalar_tensor_tensor(out=newton[:, c:c + 1], in0=inv0[:, c:c + 1], scalar=inv0[:, c:c + 1],
                                                         in1=var[:, c:c + 1], op0=ALU.mult, op1=ALU.mult)
                link(ins)
                link(nc.vector.tensor_scalar(newton[:, s], newton[:, s], -0.5, 1.5, ALU.mult, ALU.add))
                nc.vector.tensor_tensor(inv[:, s], inv0[:, s], newton[:, s], ALU.mult).then_inc(inv_ready, 1)
                dve.wait_ge(inv_ready, count)

            dve.wait_ge(gain_psum, 1)
            nc.vector.tensor_copy(gain_cols[:], acc[0][:, 0:KD]).then_inc(gain_ready, 1)
            dve.wait_ge(gain_ready, 1)
            for k in range(KD):
                if k == KD - 1:
                    mean_square(var[:, 0:NT], ss[:, 0:NT], 2, EPS).then_inc(var_ready, 1)
                xT_lo_block(k)
                split_piece(k)
            dve.wait_ge(taps_psum, 1)
            nc.vector.tensor_copy(tap_cols[:], acc[1][:, 0:3 * KC]).then_inc(taps_ready, 1)
            dve.wait_ge(taps_ready, 1)
            inverse(0, NT, 1)
            for j in range(2, 6):
                split_half(j)

            def head_out_of_psum(dst, count):
                dve.wait_ge(head_psum, count)
                for tile in range(NT):
                    ins = nc.vector.tensor_copy(dst[:, :, tile * P:(tile + 1) * P],
                                                tr[tile][:].rearrange("p (k s) -> p k s", s=P))
                ins.then_inc(head_taken, 1)

            head_out_of_psum(qT, 2)
            split_half(6)
            split_half(7)

            def tap(j, c):
                return tap_cols[:, j * KC + c:j * KC + c + 1]

            for unit in range(4, 2 * N_PROJ):
                step, t = divmod(unit, NT)
                if t == 1:
                    split_half(2 * step + 4)
                head = unit - ATT0
                if unit == 4:
                    head_out_of_psum(kT, 4)
                if 0 <= head < H:
                    if head == 0:
                        dve.wait_ge(bias_loaded, 16)
                    dve.wait_ge(scores_ready, head + 1)
                    if head >= 2:
                        dve.wait_ge(probsT_psum, head - 1)
                    for tile, cols, window in ((1, slice(0, TWO), slice(TWO - 1, None, -1)),
                                               (0, slice(TWO, ROW), slice(P - 1, None, -1))):
                        ins = nc.vector.tensor_tensor_reduce(
                            out=probs[:, head % 2, cols], in0=score_ps[:, cols], in1=bias[:, head, window],
                            scale=-SCALE, scalar=3.0e38, op0=ALU.add, op1=ALU.min,
                            accum_out=neg_max[:, tile, head:head + 1])
                    ins.then_inc(scores_biased, 1)
                if 1 <= head <= H:
                    dve.wait_ge(probsT_psum, head)
                    if head >= 3:
                        dve.wait_ge(pv_done, head - 2)
                    nc.vector.tensor_copy(probsT[:, (head - 1) % 2, :], probT_ps[:, 0:ROW]).then_inc(probsT_ready, 1)
                if step == STEP_C:
                    if t == 0:
                        dve.wait_ge(tile0_done, step + 1)
                        dve.wait_ge(head_psum, 4)
                    else:
                        dve.wait_ge(halves_used, 2 * step + 2)
                    dve.wait_ge(proj_taken[t], STEP_XIN + 1)
                    nc.vector.scalar_tensor_tensor(out=u_tok[:, t, :], in0=acc[t][:], scalar=inv[:, t:t + 1],
                                                   in1=xin_tok[:, t, :], op0=ALU.mult, op1=ALU.mult).then_inc(
                                                       proj_taken[t], 1)
                if unit == 2 * STEP_B:
                    dve.wait_ge(convT_psum, 2)
                    for tile in range(NT):
                        ins = nc.vector.tensor_copy(uT[:, :, 2 + tile * P:2 + (tile + 1) * P],
                                                    tr[tile][:].rearrange("p (k s) -> p k s", s=P))
                    ins.then_inc(uT_ready, 1)
                    dve.wait_ge(uT_ready, 1)
                if unit == 2 * STEP_B + 1:
                    dve.wait_ge(consts_ready, 2)
                    for c in range(KC):
                        ins = nc.vector.tensor_scalar(conv[:, c, :], uT[:, c, 2:2 + SEQ], tap(2, c), None, ALU.mult)
                    link(ins)
                    for j in (1, 0):
                        for c in range(KC):
                            ins = nc.vector.scalar_tensor_tensor(out=conv[:, c, :], in0=uT[:, c, j:j + SEQ],
                                                                 scalar=tap(j, c), in1=conv[:, c, :],
                                                                 op0=ALU.mult, op1=ALU.add)
                        link(ins)
                if unit == 2 * STEP_B + 3:
                    dve.wait_ge(convT_psum, 4)
                    for tile in range(NT):
                        half_conv = conv[:, :, tile * P:(tile + 1) * P]
                        ins = nc.vector.tensor_tensor(half_conv, tr[tile][:].rearrange("p (k s) -> p k s", s=P),
                                                      half_conv, ALU.mult)
                    ins.then_inc(y_ready, 1)
                    dve.wait_ge(y_hi_ready, 1)
                    nc.vector.tensor_tensor(midT_lo[:], conv, midT_hi[:].bitcast(F32), ALU.subtract).then_inc(y_lo_ready, 1)
                if unit == ATT0 + H + 2:
                    link(nc.vector.reciprocal(rden[:], den[:]))
                    dve.wait_ge(pv_done, H)
                    for tile in range(NT):
                        ins = nc.vector.tensor_tensor(att_tok[:, tile, :].rearrange("p (h d) -> p h d", h=H),
                                                      att_ps[tile][:].rearrange("p (h d) -> p h d", h=H),
                                                      rden[:, tile, :].unsqueeze(2).to_broadcast([P, H, HD]), ALU.mult)
                    ins.then_inc(att_ready, 1)
                if unit == ATT0 + H + 3:
                    for tile in range(NT):
                        cols = slice(tile * P, (tile + 1) * P)
                        dve.wait_ge(attT_hi_ready, tile + 1)
                        nc.vector.tensor_tensor(attT_lo[:, :, cols], tr[tile][:].rearrange("p (k s) -> p k s", s=P),
                                                attT_hi[:, :, cols].bitcast(F32), ALU.subtract).then_inc(attT_lo_ready, 1)
                if t == 1:
                    split_half(2 * step + 5)

            def gate(t, n):
                if t == 0:
                    dve.wait_ge(branch_done, n + 1)
                else:
                    dve.wait_ge(halves_used, J_BRANCH + 2 * n + 2)
                for b in range(2):
                    g = gates[:, t, b * D + n * W:b * D + (n + 1) * W]
                    ins = nc.vector.tensor_tensor(g, branch_ps[n][b][:], g, ALU.mult)
                ins.then_inc(gated, 1)

            gate(0, 0)
            gate(0, 1)
            split_half(J_O)
            gate(1, 0)
            inT_lo_tile(0, 1)
            split_half(J_O + 1)
            gate(1, 1)
            split_half(J_O + 2)
            split_half(J_O + 3)
            inT_lo_tile(1, 2)

            def mix_gain(t, n):
                dve.wait_ge(squared, MIX_SQUARED[t][n])
                cols = slice(n * W, (n + 1) * W)
                nc.vector.tensor_tensor(rows[:, t, cols], mix_ps[t][n][:], g_post[:, cols], ALU.mult).then_inc(mix_gained, 1)

            def residual(t):
                dve.wait_ge(mix_gained, 2 * t + 2)
                nc.vector.scalar_tensor_tensor(out=resid[:, t, :], in0=rows[:, t, :], scalar=inv[:, 2 + t:3 + t],
                                               in1=resid[:, t, :], op0=ALU.mult, op1=ALU.add).then_inc(resid_ready, 1)
                dve.wait_ge(resid_ready, t + 1)
                nc.vector.tensor_tensor(rows[:, t, :], resid[:, t, :], g_mlp, ALU.mult).then_inc(h_ready, 1)

            def mix_variance(t, n):
                if n == 0:
                    link(mean_square(var[:, 2 + t:3 + t], ss[:, 2 + 2 * t:3 + 2 * t], MIX_SQUARED[t][n], EPS))
                else:
                    mean_square(var[:, 2 + t:3 + t], ss[:, 3 + 2 * t:4 + 2 * t], MIX_SQUARED[t][n],
                                var[:, 2 + t:3 + t]).then_inc(var_ready, 1)

            dve.wait_ge(gains_loaded[0], 16)
            dve.wait_ge(gains_loaded[1], 16)
            mix_gain(0, 0)
            mix_variance(0, 0)
            mix_variance(0, 1)
            mix_gain(0, 1)
            inverse(2, 1, 2)
            residual(0)
            split_half(J_MLP)
            inT_lo_tile(0, 3)
            mix_gain(1, 0)
            mix_variance(1, 0)
            split_half(J_MLP + 1)
            mean_square(var[:, 4:5], ss[:, 6:7], RESID_SQUARED[0], EPS).then_inc(var_ready, 1)
            split_half(J_MLP + 2)
            mix_variance(1, 1)
            mix_gain(1, 1)
            inverse(4, 1, 3)
            inverse(3, 1, 4)
            residual(1)
            mean_square(var[:, 5:6], ss[:, 7:8], RESID_SQUARED[1], EPS).then_inc(var_ready, 1)
            inT_lo_tile(1, 4)
            inverse(5, 1, 5)

            def hiddenT_lo_tile(t, count):
                dve.wait_ge(hiddenT_hi, count)
                nc.vector.tensor_tensor(midT_lo[:, :, t * P:(t + 1) * P], tr[t][:].rearrange("p (k s) -> p k s", s=P),
                                        midT_hi[:, :, t * P:(t + 1) * P].bitcast(F32),
                                        ALU.subtract).then_inc(hiddenT_lo, 1)

            split_half(J_MLP + 4)
            hiddenT_lo_tile(0, 1)
            split_half(J_MLP + 5)
            hiddenT_lo_tile(1, 2)
            split_half(J_MLP + 6)
            split_half(J_MLP + 7)
            hiddenT_lo_tile(0, 3)
            hiddenT_lo_tile(1, 4)
            with dve.Fori(0, N_FF - 2) as i:
                for h in range(4):
                    split_lo(4 * i + J_MLP + 8 + h, h)
                hiddenT_lo_tile(0, 2 * i + 5)
                hiddenT_lo_tile(1, 2 * i + 6)
            dve.wait_ge(gains_loaded[2], 16)

            def down_gain(t, lo, hi):
                n = lo // W
                nc.vector.tensor_tensor(rows[:, t, lo:hi], down_ps[t][n][:, lo - n * W:hi - n * W], g_last[:, lo:hi],
                                        ALU.mult).then_inc(down_gained, 1)

            def finish(t, n, count):
                dve.wait_ge(down_gained, count)
                cols = slice(n * W, (n + 1) * W)
                nc.vector.scalar_tensor_tensor(out=rows[:, t, cols], in0=rows[:, t, cols], scalar=inv[:, 6 + t:7 + t],
                                               in1=resid[:, t, cols], op0=ALU.mult, op1=ALU.add).then_inc(out_ready, 1)

            for t in range(NT):
                v, part = var[:, 6 + t:7 + t], ss[:, 8 + 2 * t:10 + 2 * t]
                link(mean_square(v, part[:, 0:1], 9 + 2 * t, EPS))
                down_gain(t, 0, W)
                mean_square(v, part[:, 1:2], 10 + 2 * t, v).then_inc(var_ready, 1)
                down_gain(t, W, W + W // 2)
                inverse(6 + t, 1, 6 + t)
                finish(t, 0, 3 * t + 1)
                down_gain(t, W + W // 2, D)
                finish(t, 1, 3 * t + 3)

        @block.tensor
        def _(pe):
            def product(bank, a_hi, a_lo, k, t, slot, off, start, stop):
                hi, lo = a_hi[:, k, t * P:(t + 1) * P], a_lo[:, k, t * P:(t + 1) * P]
                b_hi, b_lo = w_hi[:, slot, off:off + W], w_lo[:, slot, off:off + W]
                nc.tensor.matmul(bank[:], hi, b_hi, start=start, stop=False)
                nc.tensor.matmul(bank[:], hi, b_lo, start=False, stop=False)
                return nc.tensor.matmul(bank[:], lo, b_hi, start=False, stop=stop)

            def wide_unit(bank, t, slot0, first_half, done=None, at=None):
                for k in range(KD):
                    if at and k in at:
                        at[k]()
                    elif t == 0 and k % HALF_K == 0:
                        pe.wait_ge(half_lo, first_half + k // HALF_K + 1)
                    last = product(bank, inT_hi, inT_lo, k, t, slot0 + k // HALF_K, k % HALF_K * W, k == 0, k == KD - 1)
                    if t == 1 and k % HALF_K == HALF_K - 1 and (done is None or k < KD - 1):
                        last.then_inc(halves_used, 1)
                if done is not None:
                    last.then_inc(done, 1)

            def transpose_rows(src, t, done):
                for k in range(KD):
                    last = nc.tensor.transpose(tr[k // 4][:, k % 4 * P:(k % 4 + 1) * P],
                                               src[:, t, k * P:(k + 1) * P], ident[:])
                last.then_inc(done, 1)

            def transpose_cols(src, t, done):
                for k in range(KC):
                    last = nc.tensor.transpose(tr[t][:, k * P:(k + 1) * P], src[:, t, k * P:(k + 1) * P], ident[:])
                last.then_inc(done, 1)

            def transpose_x(k):
                if k % 2 == 0:
                    pe.wait_ge(x_loaded[k // 2], 16)
                for t in range(NT):
                    last = nc.tensor.transpose(xT_ps[k % 4][:, t * P:(t + 1) * P], resid[:, t, k * P:(k + 1) * P], ident[:])
                last.then_inc(xT_psum, 1)

            def keep_clock_up(n):
                for _ in range(n):
                    nc.tensor.transpose(acc[1][:, 0:P], ident[:], ident[:])

            pe.wait_ge(consts_ready, 1)
            keep_clock_up(9)
            transpose_x(0)
            pe.wait_ge(gain_loaded, 16)
            nc.tensor.transpose(acc[0][:, 0:KD], gain_rows, ident[0:KD, 0:KD]).then_inc(gain_psum, 1)
            transpose_x(1)
            keep_clock_up(5)

            def pair(ps, k, slot, hi_operand, lo_weights, stop=False):
                b = (w_lo if lo_weights else w_hi)[:, slot, k % HALF_K * W:(k % HALF_K + 1) * W]
                for t in range(NT):
                    a = (inT_hi if hi_operand else inT_lo)[:, k, t * P:(t + 1) * P]
                    last = nc.tensor.matmul(ps[t][:], a, b, start=k == 0 and hi_operand and not lo_weights, stop=stop)
                    if stop and t == 0:
                        last.then_inc(tile0_done, 1)
                return last

            for k in range(KD):
                slot = k // HALF_K
                pe.wait_ge(xT_hi, k + 1)
                pe.wait_ge(piece_hi, k + 1)
                pair(proj_ps[0], k, slot, True, False)
                pe.wait_ge(xT_lo, k + 1)
                pair(proj_ps[0], k, slot, False, False)
                if k % HALF_K < HALF_K - 1:
                    pe.wait_ge(piece_lo, k + 1 - slot)
                else:
                    pe.wait_ge(half_lo, slot + 1)
                last = pair(proj_ps[0], k, slot, True, True, stop=k == KD - 1)
                if k % HALF_K == HALF_K - 1:
                    last.then_inc(halves_used, 1)
                if k == 0:
                    transpose_x(2)
                if k + 3 < KD:
                    transpose_x(k + 3)
                if k == KD - 2:
                    pe.wait_ge(taps_loaded, 16)
                    nc.tensor.transpose(acc[1][:, 0:3 * KC], tap_rows, ident[0:3 * KC, 0:3 * KC]).then_inc(taps_psum, 1)
            pe.wait_ge(taps_ready, 1)
            for h in range(2):
                j = 2 + h
                ks = range(h * HALF_K, (h + 1) * HALF_K)
                pe.wait_ge(half_hi, j - 1)
                for k in ks:
                    pair(proj_ps[1], k, j, True, False)
                    pair(proj_ps[1], k, j, False, False)
                pe.wait_ge(half_lo, j + 1)
                for k in ks:
                    last = pair(proj_ps[1], k, j, True, True, stop=k == KD - 1)
                last.then_inc(halves_used, 1)
                if h == 0:
                    for tile in range(NT):
                        pe.wait_ge(proj_taken[tile], 1)
                        transpose_cols(q_tok, tile, head_psum)

            for unit in range(4, 2 * N_PROJ):
                step, t = divmod(unit, NT)
                former = max(s for s in range(step) if proj_ps[s] is proj_ps[step])
                pe.wait_ge(proj_taken[t], former + 1)
                wide_unit(proj_ps[step][t], t, 2 * step % SLOTS, 2 * step, done=tile0_done if t == 0 else None)
                if unit == 4:
                    pe.wait_ge(head_taken, 1)
                    for tile in range(NT):
                        pe.wait_ge(proj_taken[tile], 2)
                        transpose_cols(k_tok, tile, head_psum)
                head = unit - ATT0
                if 0 <= head < H:
                    if head == 0:
                        pe.wait_ge(head_taken, 2)
                    else:
                        pe.wait_ge(scores_biased, head)
                    part, pair = slice(HD * (head % 2), HD * (head % 2) + HD), head // 2
                    nc.tensor.matmul(score_ps[:, 0:TWO], qT[part, pair, P:TWO], kT[part, pair, :], start=True, stop=True)
                    nc.tensor.matmul(score_ps[:, TWO:ROW], qT[part, pair, 0:P], kT[part, pair, 0:P],
                                     start=True, stop=True).then_inc(scores_ready, 1)
                if 1 <= head <= H:
                    pe.wait_ge(probs_ready, head)
                    if head >= 2:
                        pe.wait_ge(probsT_ready, head - 1)
                    for b in range(3):
                        last = nc.tensor.transpose(probT_ps[:, b * P:(b + 1) * P],
                                                   probs[:, (head - 1) % 2, b * P:(b + 1) * P], ident[:])
                    last.then_inc(probsT_psum, 1)
                if 2 <= head <= H + 1:
                    h = head - 2
                    cols = slice(h * HD, (h + 1) * HD)
                    pe.wait_ge(probsT_ready, h + 1)
                    if h == 0:
                        pe.wait_ge(proj_taken[1], 3)
                        pe.wait_ge(proj_taken[0], 3)
                    nc.tensor.matmul(att_ps[1][:, cols], probsT[:, h % 2, 0:P], v_tok[:, 0, cols], start=True, stop=False)
                    nc.tensor.matmul(att_ps[1][:, cols], probsT[:, h % 2, P:TWO], v_tok[:, 1, cols], start=False, stop=True)
                    nc.tensor.matmul(att_ps[0][:, cols], probsT[:, h % 2, TWO:ROW], v_tok[:, 0, cols],
                                     start=True, stop=True).then_inc(pv_done, 1)
                if unit == 2 * STEP_B:
                    for tile in range(NT):
                        pe.wait_ge(proj_taken[tile], STEP_C + 1)
                        transpose_cols(u_tok, tile, convT_psum)
                if unit == 2 * STEP_B + 2:
                    pe.wait_ge(uT_ready, 1)
                    for tile in range(NT):
                        pe.wait_ge(proj_taken[tile], STEP_B + 1)
                        transpose_cols(gb_tok, tile, convT_psum)
                if unit == ATT0 + H + 3:
                    pe.wait_ge(y_ready, 1)
                    pe.wait_ge(att_ready, 1)
                    for tile in range(NT):
                        transpose_cols(att_tok, tile, attT_psum)
            def branch_unit(t, n):
                for b, (a_hi, a_lo) in enumerate(((midT_hi, midT_lo), (attT_hi, attT_lo))):
                    j = J_BRANCH + 2 * n + b
                    if t == 0:
                        pe.wait_ge(half_lo, j + 1)
                    for k in range(KC):
                        last = product(branch_ps[n][b], a_hi, a_lo, k, t, j % SLOTS, k * W, k == 0, k == KC - 1)
                    if t == 1:
                        last.then_inc(halves_used, 1)
                if t == 0:
                    last.then_inc(branch_done, 1)

            pe.wait_ge(y_lo_ready, 1)
            pe.wait_ge(attT_lo_ready, 2)
            pe.wait_ge(probsT_ready, H)
            branch_unit(0, 0)
            pe.wait_ge(proj_taken[0], N_PROJ)
            pe.wait_ge(proj_taken[1], N_PROJ)
            branch_unit(0, 1)
            pe.wait_ge(gated, 1)
            branch_unit(1, 0)
            pe.wait_ge(m_ready, 2)
            transpose_rows(rows, 0, inT_psum)
            pe.wait_ge(gated, 2)
            branch_unit(1, 1)

            def transpose_m1():
                pe.wait_ge(half_lo, J_O + 4)
                pe.wait_ge(m_ready, 4)
                pe.wait_ge(inT_lo_ready, 2)
                transpose_rows(rows, 1, inT_psum)

            def transpose_h0():
                pe.wait_ge(h_ready, 1)
                transpose_rows(rows, 0, inT_psum)

            def transpose_h1():
                pe.wait_ge(h_ready, 2)
                transpose_rows(rows, 1, inT_psum)

            pe.wait_ge(gated, 3)
            pe.wait_ge(inT_lo_ready, 2)
            wide_unit(mix_ps[0][0], 0, J_O % SLOTS, J_O, done=tile0_done)
            wide_unit(mix_ps[0][1], 0, (J_O + 2) % SLOTS, J_O + 2, done=tile0_done, at={HALF_K: transpose_m1})
            pe.wait_ge(gated, 4)
            pe.wait_ge(inT_lo_ready, 4)
            wide_unit(mix_ps[1][0], 1, J_O % SLOTS, J_O)
            transpose_h0()
            wide_unit(mix_ps[1][1], 1, (J_O + 2) % SLOTS, J_O + 2)

            def up_unit(t, bank, slot0, first_half, at=None):
                wide_unit(bank, t, slot0, first_half, done=tile0_done if t == 0 else None, at=at)

            def down_unit(t, slot0, first_half, first=False, last_group=False):
                def part(k, n, stop=False):
                    return product(down_ps[t][n], midT_hi, midT_lo, k, t, slot0 + k // 2, k % 2 * D + n * W,
                                   first and k == 0, stop)

                for h in range(2):
                    if t == 0:
                        pe.wait_ge(half_lo, first_half + h + 1)
                    if last_group:
                        continue
                    for k in (2 * h, 2 * h + 1):
                        for n in range(2):
                            ins = part(k, n)
                    if t == 1:
                        ins.then_inc(halves_used, 1)
                if last_group:
                    for n in range(2):
                        for k in range(KC):
                            ins = part(k, n, stop=k == KC - 1)
                        ins.then_inc(down_done, 1)

            def transpose_hidden(src, t, count):
                pe.wait_ge(hidden_ready, count)
                transpose_cols(src, t, hiddenT_psum)

            pe.wait_ge(inT_lo_ready, 6)
            up_unit(0, score_ps, J_MLP % SLOTS, J_MLP)
            up_unit(0, probT_ps, (J_MLP + 2) % SLOTS, J_MLP + 2,
                    at={HALF_K: lambda: pe.wait_ge(early_lo, 1),
                        HALF_K + 1: transpose_h1,
                        HALF_K + 2: lambda: pe.wait_ge(half_lo, J_MLP + 4)})
            pe.wait_ge(inT_lo_ready, 7)
            up_unit(1, acc[0], J_MLP % SLOTS, J_MLP, at={HALF_K: lambda: pe.wait_ge(inT_lo_ready, 8)})
            transpose_hidden(hidden0, 0, 1)
            up_unit(1, acc[1], (J_MLP + 2) % SLOTS, J_MLP + 2, at={HALF_K: lambda: transpose_hidden(hidden0, 1, 3)})
            pe.wait_ge(hiddenT_lo, 1)
            down_unit(0, 0, J_MLP + 4, first=True)
            transpose_hidden(hidden, 0, 2)
            pe.wait_ge(hiddenT_lo, 2)
            pe.wait_ge(relu_done, 2)
            down_unit(1, 0, J_MLP + 4, first=True)
            transpose_hidden(hidden, 1, 4)
            with pe.Fori(0, N_FF - 2) as i:
                for t in range(NT):
                    pe.wait_ge(relu_done, 2 * i + 3 + t)
                    up_unit(t, acc[t], 2, 4 * i + J_MLP + 6)
                for t in range(NT):
                    pe.wait_ge(hiddenT_lo, 2 * i + 3 + t)
                    down_unit(t, 0, 4 * i + J_MLP + 8)
                    transpose_hidden(hidden, t, 2 * i + 5 + t)
            for t in range(NT):
                pe.wait_ge(hiddenT_lo, 2 * N_FF - 1 + t)
                down_unit(t, 2, N_HALVES - 2, last_group=True)


_INS = ["x", "ln_mix_pre", "w_in", "conv_w", "w_conv_out", "w_attn_out", "rel_bias", "w_o",
        "ln_mix_post", "ln_mlp_pre", "w_mlp_in", "w_mlp_out", "ln_mlp_post"]
_OUTS = [((1, 256, 1024), "float32")]


def kernel(**inputs):
    import numpy as _np
    import concourse.bacc as _bacc
    from concourse import mybir as _mybir
    from concourse.bass_utils import run_bass_kernel_spmd as _run

    nc = _bacc.Bacc("TRN2", target_bir_lowering=False, num_devices=1)
    arrays, args = {}, []
    for name in _INS:
        a = _np.ascontiguousarray(inputs[name])
        arrays[f"in_{name}_dram"] = a
        args.append(nc.dram_tensor(f"in_{name}_dram", a.shape, _mybir.dt.from_np(a.dtype), kind="ExternalInput").ap())
    for i, (shape, dtype) in enumerate(_OUTS):
        dt = _mybir.dt.from_np(_np.dtype(dtype))
        args.append(nc.dram_tensor(f"out_{i}_dram", shape, dt, kind="ExternalOutput").ap())
    hybrid_layer(nc, *args)
    r = _run(nc, [arrays], core_ids=[0])
    return r.results[0]["out_0_dram"]
```
